# Optimizing a Trainium2 kernel written in Bass

```python
import math
import jax
import jax.numpy as jnp
from jax import lax
import numpy as np

D_MODEL = 1024
BATCH = 1
SEQ = 128
DEPTH = 2
DEC_BATCH = 1
DEC_SEQ = 256
PAST_LEN = 128

GRID_W = 64
N_MIXERS = 2
N_HGRN_LAYERS = (DEPTH + 1) // 2
N_ATTN_LAYERS = DEPTH // 2
HGRN_HEADS = D_MODEL // 128
HGRN_DK = D_MODEL // HGRN_HEADS
HGRN_DV = D_MODEL // HGRN_HEADS
HGRN_CHUNK = 32
DIFF_HEADS = 8
DIFF_QK_DIM = D_MODEL // (2 * DIFF_HEADS)
DIFF_V_DIM = D_MODEL // DIFF_HEADS
ROPE_THETA = 10000.0
Q_BLOCK = 128
MOE_GROUPS = 4
MOE_EXPERTS_PER_GROUP = 4
MOE_N_EXPERTS = MOE_GROUPS * MOE_EXPERTS_PER_GROUP
MOE_TOP_K = 2
MOE_D_FF = D_MODEL // 2
EPS = 1e-6

kernel_name = "hybrid_hgrn2_diffattn_hmoe_diffusion_step"

def rmsnorm(x, g):
    xf = x.astype(jnp.float32)
    y = xf * lax.rsqrt(jnp.mean(xf * xf, axis=-1, keepdims=True) + EPS)
    return (y * g.astype(jnp.float32)).astype(x.dtype)

def modulation(cvec, w_ada, b_ada):
    m = jax.nn.silu(cvec) @ w_ada + b_ada
    return jnp.split(m, 6, axis=-1)

def hgrn2_chunk_scan(q, k, v, logf, s0):
    T = q.shape[-2]
    n = T // HGRN_CHUNK

    def chunks(a):
        a = a.reshape(a.shape[:-2] + (n, HGRN_CHUNK, a.shape[-1]))
        return jnp.moveaxis(a, -3, 0)

    causal = jnp.tril(jnp.ones((HGRN_CHUNK, HGRN_CHUNK), dtype=bool))[:, :, None]

    def step(S, inp):
        qc, kc, vc, gc = inp
        b = jnp.cumsum(gc, axis=-2)
        rel = b[..., :, None, :] - b[..., None, :, :]
        dec = jnp.exp(jnp.where(causal, rel, -jnp.inf))
        att = jnp.einsum('...td,...sd,...tsd->...ts', qc, kc, dec)
        o = att @ vc + jnp.einsum('...td,...dv->...tv', qc * jnp.exp(b), S)
        b_last = b[..., -1:, :]
        S_new = (jnp.exp(b_last[..., 0, :])[..., None] * S
                 + jnp.einsum('...sd,...sv->...dv', kc * jnp.exp(b_last - b), vc))
        return S_new, o

    s_fin, o = lax.scan(step, s0, (chunks(q), chunks(k), chunks(v), chunks(logf)))
    o = jnp.moveaxis(o, 0, -3)
    return o.reshape(o.shape[:-3] + (T, o.shape[-1])), s_fin

def hgrn2_mixer(u, w_in, lb, onorm_g, w_out, s0):
    Bn, T, _ = u.shape
    q, inp, zf, zb, g = jnp.split(u @ w_in, 5, axis=-1)

    def heads(a):
        return a.reshape(Bn, T, HGRN_HEADS, -1).transpose(0, 2, 1, 3).astype(jnp.float32)

    def bidir(a_f, a_b):
        return jnp.stack([heads(a_f), jnp.flip(heads(a_b), axis=2)], axis=1)

    z = bidir(zf, zb)
    lbd = lb.astype(jnp.float32).reshape(2, HGRN_HEADS, 1, HGRN_DK)
    logf = jnp.log(lbd + (1.0 - lbd) * jax.nn.sigmoid(z))
    k = (1.0 - lbd) * jax.nn.sigmoid(-z)
    o, s_fin = hgrn2_chunk_scan(bidir(q, q), k, bidir(inp, inp), logf, s0.astype(jnp.float32))
    o = o[:, 0] + jnp.flip(o[:, 1], axis=2)
    o = o.transpose(0, 2, 1, 3).astype(u.dtype)
    o = rmsnorm(o, onorm_g) * jax.nn.silu(g.reshape(Bn, T, HGRN_HEADS, HGRN_DV))
    return o.reshape(Bn, T, D_MODEL) @ w_out, s_fin.astype(u.dtype)

def diff_attn_qkv(u, w_qkv, qn_g, kn_g):
    Bn, T, _ = u.shape
    q, k, v = jnp.split(u @ w_qkv, 3, axis=-1)
    q = rmsnorm(q.reshape(Bn, T, DIFF_HEADS, 2, DIFF_QK_DIM), qn_g)
    k = rmsnorm(k.reshape(Bn, T, DIFF_HEADS, 2, DIFF_QK_DIM), kn_g)
    v = v.reshape(Bn, T, DIFF_HEADS, DIFF_V_DIM)
    return q, k, v

def diff_lambda(lam_p, layer_idx):
    lf = lam_p.astype(jnp.float32)
    lam_init = 0.8 - 0.6 * math.exp(-0.3 * layer_idx)
    lam = jnp.exp(jnp.sum(lf[0] * lf[1])) - jnp.exp(jnp.sum(lf[2] * lf[3])) + lam_init
    return lam, lam_init

def diff_attention(q, k, v, lam):
    Bn, Tq = q.shape[0], q.shape[1]
    nb = Tq // Q_BLOCK
    qb = jnp.moveaxis(q.reshape(Bn, nb, Q_BLOCK, DIFF_HEADS, 2, DIFF_QK_DIM), 1, 0)
    scale = DIFF_QK_DIM ** -0.5

    def block(qi):
        s = jnp.einsum('bqhcd,bkhcd->bhcqk', qi, k).astype(jnp.float32) * scale
        p = jax.nn.softmax(s, axis=-1)
        a = (p[:, :, 0] - lam * p[:, :, 1]).astype(v.dtype)
        return jnp.einsum('bhqk,bkhv->bqhv', a, v)

    o = lax.map(block, qb)
    return jnp.moveaxis(o, 0, 1).reshape(Bn, Tq, DIFF_HEADS, DIFF_V_DIM)

def diff_attn_out(o, subln_g, lam_init, w_out):
    Bn, T = o.shape[0], o.shape[1]
    o = rmsnorm(o, subln_g) * (1.0 - lam_init)
    return o.reshape(Bn, T, D_MODEL) @ w_out

def rope_1d(x, ang):
    x1, x2 = jnp.split(x, 2, axis=-1)
    c = jnp.cos(ang).astype(x.dtype)
    s = jnp.sin(ang).astype(x.dtype)
    return jnp.concatenate([x1 * c - x2 * s, x2 * c + x1 * s], axis=-1)

def axial_rope(x, ang_row, ang_col):
    xr, xc = jnp.split(x, 2, axis=-1)
    return jnp.concatenate([rope_1d(xr, ang_row), rope_1d(xc, ang_col)], axis=-1)

def hier_moe(u, w_group, b_group, w_expert, b_expert, w_gate, w_up, w_down):
    shp = u.shape
    xt = u.reshape(-1, D_MODEL)
    g_prob = jax.nn.softmax((xt @ w_group + b_group).astype(jnp.float32), axis=-1)
    g_w, g_idx = lax.top_k(g_prob, 1)
    e_logits = (xt @ w_expert + b_expert).astype(jnp.float32).reshape(-1, MOE_GROUPS, MOE_EXPERTS_PER_GROUP)
    e_sel = jnp.take_along_axis(e_logits, g_idx[:, :, None], axis=1)[:, 0]
    e_w, e_idx = lax.top_k(jax.nn.softmax(e_sel, axis=-1), MOE_TOP_K)
    e_w = e_w / jnp.sum(e_w, axis=-1, keepdims=True)
    expert_id = g_idx * MOE_EXPERTS_PER_GROUP + e_idx
    combine = jnp.sum(jax.nn.one_hot(expert_id, MOE_N_EXPERTS, dtype=jnp.float32)
                      * (g_w * e_w)[..., None], axis=1)
    h = jax.nn.silu(jnp.einsum('nd,edf->nef', xt, w_gate)) * jnp.einsum('nd,edf->nef', xt, w_up)
    h = h * combine.astype(h.dtype)[:, :, None]
    y = jnp.einsum('nef,efd->nd', h, w_down)
    return y.reshape(shp)

def setup_inputs(seed: int = 0) -> dict:
    key = jax.random.key(seed)
    ks = jax.random.split(key, 32)
    f32 = jnp.float32
    D = D_MODEL

    def nrm(k, shape, scale):
        return jax.random.normal(k, shape, f32) * scale

    return {
        "x_prompt": nrm(ks[0], (BATCH, SEQ, D), 1.0),
        "x_sample": nrm(ks[1], (DEC_BATCH, DEC_SEQ, D), 1.0),
        "c": nrm(ks[2], (DEC_BATCH, D), 1.0),
        "cache_k": nrm(ks[3], (DEC_BATCH, N_ATTN_LAYERS, PAST_LEN, DIFF_HEADS, 2, DIFF_QK_DIM), 1.0),
        "cache_v": nrm(ks[4], (DEC_BATCH, N_ATTN_LAYERS, PAST_LEN, DIFF_HEADS, DIFF_V_DIM), 1.0),
        "state_hgrn": nrm(ks[5], (DEC_BATCH, N_HGRN_LAYERS, 2, HGRN_HEADS, HGRN_DK, HGRN_DV), 0.5),
        "c_ctx": nrm(ks[6], (D,), 1.0),
        "norm_g": 1.0 + nrm(ks[7], (DEPTH, 2, D), 0.01),
        "w_ada": nrm(ks[8], (DEPTH, D, 6 * D), 0.5 * D ** -0.5),
        "b_ada": nrm(ks[9], (DEPTH, 6 * D), 0.01),
        "hgrn_w_in": nrm(ks[10], (N_HGRN_LAYERS, D, 5 * D), D ** -0.5),
        "hgrn_lb_logits": nrm(ks[11], (N_HGRN_LAYERS, 2, D), 0.5),
        "hgrn_onorm_g": 1.0 + nrm(ks[12], (N_HGRN_LAYERS, HGRN_DV), 0.01),
        "hgrn_w_out": nrm(ks[13], (N_HGRN_LAYERS, D, D), D ** -0.5),
        "attn_w_qkv": nrm(ks[14], (N_ATTN_LAYERS, D, 3 * D), D ** -0.5),
        "attn_qn_g": 1.0 + nrm(ks[15], (N_ATTN_LAYERS, DIFF_QK_DIM), 0.01),
        "attn_kn_g": 1.0 + nrm(ks[16], (N_ATTN_LAYERS, DIFF_QK_DIM), 0.01),
        "attn_lambda": nrm(ks[17], (N_ATTN_LAYERS, 4, DIFF_QK_DIM), 0.1),
        "attn_subln_g": 1.0 + nrm(ks[18], (N_ATTN_LAYERS, DIFF_V_DIM), 0.01),
        "attn_w_out": nrm(ks[19], (N_ATTN_LAYERS, D, D), D ** -0.5),
        "moe_w_group": nrm(ks[20], (DEPTH, D, MOE_GROUPS), D ** -0.5),
        "moe_b_group": nrm(ks[21], (DEPTH, MOE_GROUPS), 0.01),
        "moe_w_expert": nrm(ks[22], (DEPTH, D, MOE_N_EXPERTS), D ** -0.5),
        "moe_b_expert": nrm(ks[23], (DEPTH, MOE_N_EXPERTS), 0.01),
        "moe_w_gate": nrm(ks[24], (DEPTH, MOE_N_EXPERTS, D, MOE_D_FF), D ** -0.5),
        "moe_w_up": nrm(ks[25], (DEPTH, MOE_N_EXPERTS, D, MOE_D_FF), D ** -0.5),
        "moe_w_down": nrm(ks[26], (DEPTH, MOE_N_EXPERTS, MOE_D_FF, D), MOE_D_FF ** -0.5),
    }

def reference(x_prompt, x_sample, c, cache_k, cache_v, state_hgrn, c_ctx,
              norm_g, w_ada, b_ada,
              hgrn_w_in, hgrn_lb_logits, hgrn_onorm_g, hgrn_w_out,
              attn_w_qkv, attn_qn_g, attn_kn_g, attn_lambda, attn_subln_g, attn_w_out,
              moe_w_group, moe_b_group, moe_w_expert, moe_b_expert,
              moe_w_gate, moe_w_up, moe_w_down):
    Bp = x_prompt.shape[0]
    t_lat = x_sample.shape[1]
    rows = t_lat // GRID_W
    row = jnp.repeat(jnp.arange(rows), GRID_W).astype(jnp.float32)
    col = jnp.tile(jnp.arange(GRID_W), rows).astype(jnp.float32)
    half = DIFF_QK_DIM // 2
    inv_freq = ROPE_THETA ** (-jnp.arange(0, half, 2, dtype=jnp.float32) / half)
    ang_row = (row[:, None] * inv_freq).reshape(t_lat, 1, 1, -1)
    ang_col = (col[:, None] * inv_freq).reshape(t_lat, 1, 1, -1)
    lbs = jnp.cumsum(jax.nn.softmax(hgrn_lb_logits.astype(jnp.float32), axis=0), axis=0)
    lbs = lbs - lbs[0:1]

    xp, xs = x_prompt, x_sample
    new_k, new_v, new_s = [], [], []
    for i in range(DEPTH):
        j = i // N_MIXERS
        sh1p, sc1p, g1p, sh2p, sc2p, g2p = modulation(c_ctx, w_ada[i], b_ada[i])
        sh1s, sc1s, g1s, sh2s, sc2s, g2s = [m[:, None, :] for m in modulation(c, w_ada[i], b_ada[i])]
        hp = rmsnorm(xp, norm_g[i, 0]) * (1.0 + sc1p) + sh1p
        hs = rmsnorm(xs, norm_g[i, 0]) * (1.0 + sc1s) + sh1s
        if i % N_MIXERS == 0:
            s0 = jnp.zeros((Bp, 2, HGRN_HEADS, HGRN_DK, HGRN_DV), jnp.float32)
            yp, sp = hgrn2_mixer(hp, hgrn_w_in[j], lbs[j], hgrn_onorm_g[j], hgrn_w_out[j], s0)
            ys, _ = hgrn2_mixer(hs, hgrn_w_in[j], lbs[j], hgrn_onorm_g[j], hgrn_w_out[j], state_hgrn[:, j])
            new_s.append(sp)
        else:
            lam, lam_init = diff_lambda(attn_lambda[j], i)
            qp, kp, vp = diff_attn_qkv(hp, attn_w_qkv[j], attn_qn_g[j], attn_kn_g[j])
            yp = diff_attn_out(diff_attention(qp, kp, vp, lam), attn_subln_g[j], lam_init, attn_w_out[j])
            qs, ks_, vs = diff_attn_qkv(hs, attn_w_qkv[j], attn_qn_g[j], attn_kn_g[j])
            qs = axial_rope(qs, ang_row, ang_col)
            ks_ = axial_rope(ks_, ang_row, ang_col)
            k_all = jnp.concatenate([ks_, cache_k[:, j]], axis=1)
            v_all = jnp.concatenate([vs, cache_v[:, j]], axis=1)
            ys = diff_attn_out(diff_attention(qs, k_all, v_all, lam), attn_subln_g[j], lam_init, attn_w_out[j])
            new_k.append(kp)
            new_v.append(vp)
        xp = xp + g1p * yp
        xs = xs + g1s * ys
        hp = rmsnorm(xp, norm_g[i, 1]) * (1.0 + sc2p) + sh2p
        hs = rmsnorm(xs, norm_g[i, 1]) * (1.0 + sc2s) + sh2s
        xp = xp + g2p * hier_moe(hp, moe_w_group[i], moe_b_group[i], moe_w_expert[i], moe_b_expert[i],
                                 moe_w_gate[i], moe_w_up[i], moe_w_down[i])
        xs = xs + g2s * hier_moe(hs, moe_w_group[i], moe_b_group[i], moe_w_expert[i], moe_b_expert[i],
                                 moe_w_gate[i], moe_w_up[i], moe_w_down[i])

    return (xp, xs, jnp.stack(new_k, axis=1), jnp.stack(new_v, axis=1), jnp.stack(new_s, axis=1))


_drawn_inputs = setup_inputs


def setup_inputs(seed=0):
    import zlib

    import numpy as np

    out = dict(_drawn_inputs(seed))
    spreads = {}
    factors = {'state_hgrn': 4.336,
     'norm_g': 4.727,
     'b_ada': 2.819,
     'hgrn_onorm_g': 6.607,
     'attn_qn_g': 8.0,
     'attn_kn_g': 4.727,
     'attn_lambda': 5.179,
     'attn_subln_g': 7.648,
     'moe_b_group': 8.0,
     'moe_b_expert': 7.821}
    for name, (base, spread) in spreads.items():
        noise = np.random.default_rng([zlib.crc32(name.encode()), seed]).standard_normal(out[name].shape)
        drawn = base * np.exp(spread * noise) if base else spread * noise
        out[name] = jnp.asarray(drawn.astype(out[name].dtype))
    for name, factor in factors.items():
        out[name] = (out[name] * factor).astype(out[name].dtype)
    return out
```

```python
from contextlib import ExitStack

import numpy as np

import concourse.bass as bass
from concourse import mybir

ALU = mybir.AluOpType
ACT = mybir.ActivationFunctionType
F32 = mybir.dt.float32
I32 = mybir.dt.int32
U8 = mybir.dt.uint8
X_AXIS = mybir.AxisListType.X

P = 128
D = 1024
KC = D // P
T = 3
TOK = T * P
HEADS = 8
LEVELS = 7
EXPERTS = 16
GROUPS = 4
SLOTS = 64
PAIRS = EXPERTS // 2
DFF = 512
EPS = 1e-6
DQK = 64
GRID_W = 64
LAYER_IDX = 1
LAM_INIT = 0.8 - 0.6 * float(np.exp(-0.3 * LAYER_IDX))
NOT_HERE = 1000.0
RING = 6
COND = [(0, 0, 1), (1, 1, 3)]

CONST = {}


def const_layout():
    at = 0
    for name, n in (("ident", P), ("tri", P), ("iota", P), ("ones", P), ("selcol", 2),
                    ("rope", 2 * 2 * DQK), ("over", 5), ("first", 4), ("pad", 1)):
        CONST[name] = (at, at + n)
        at += n
    return at


N_CONST = const_layout()


def shape_constants():
    c = np.zeros((P, N_CONST), np.float32)

    def put(name, a):
        lo, hi = CONST[name]
        c[:, lo:hi] = np.asarray(a, np.float32).reshape(P, hi - lo)

    i = np.arange(P)
    put("ident", np.eye(P))
    put("tri", i[:, None] < i[None, :])
    put("iota", np.tile(i % SLOTS, (P, 1)))
    put("ones", np.ones((P, P)))
    of_cond = np.stack([(i % 32 == n) for n in range(2)], 1)
    put("selcol", of_cond)
    half = DQK // 2
    inv = (np.float32(10000.0) ** (-np.arange(0, half, 2, dtype=np.float32) / np.float32(half))).astype(np.float32)
    rope = np.zeros((P, 2, 2, 2, 2, half // 2), np.float64)
    for t in range(2):
        pos = t * P + i
        for rc, coord in enumerate((pos // GRID_W, pos % GRID_W)):
            ang = (coord.astype(np.float32)[:, None] * inv).astype(np.float32).astype(np.float64)
            rope[:, t, 0, rc, 0] = rope[:, t, 0, rc, 1] = np.cos(ang)
            rope[:, t, 1, rc, 0] = -np.sin(ang)
            rope[:, t, 1, rc, 1] = np.sin(ang)
    put("rope", rope)
    put("over", np.tile(np.arange(1, 6) * SLOTS, (P, 1)))
    put("first", np.tile([4, 3, 2, 1], (P, 1)))
    masks = np.zeros((P, 2 * LEVELS + 1, P), np.float32)
    s, t = i[:, None], i[None, :]
    for n in range(LEVELS):
        half_block = 1 << n
        same = s // (2 * half_block) == t // (2 * half_block)
        masks[:, n] = same & (s // half_block % 2 == 0) & (t // half_block % 2 == 1)
        masks[:, LEVELS + n] = same & (s // half_block % 2 == 1) & (t // half_block % 2 == 0)
    masks[:, 2 * LEVELS] = np.eye(P)
    return c, masks.reshape(P, -1)


class Chain:

    def __init__(self, eng, sem):
        self.eng, self.sem, self.n, self.turn = eng, sem, 0, 0

    def __call__(self, ins):
        self.n += 1
        ins.then_inc(self.sem, 1)
        self.eng.wait_ge(self.sem, self.turn + self.n)


def trunk(nc, a, out):
    with ExitStack() as ctx:
        def sb(name, shape, dt=F32, within=ctx):
            return within.enter_context(nc.sbuf_tensor(name, shape, dt))

        def sem(name):
            return ctx.enter_context(nc.semaphore(name))

        ring = [sb(f"ring{s}", [P, 4096]) for s in range(RING)]
        x = sb("x", [P, T, D])
        xn = sb("xn", [P, T, D])
        uT = sb("uT", [P, KC, TOK])
        gates = sb("gates", [P, 2, D])
        con = sb("con", [P, N_CONST])
        masks = sb("masks", [P, 2 * LEVELS + 1, P], U8)
        small_rows = sb("small_rows", [32, P])
        bias_rows = sb("bias_rows", [96, P])
        small = sb("small", [P, 32])
        bias_col = sb("bias_col", [P, 96])
        c_raw = sb("c_raw", [P, 2, KC])
        c_sig = sb("c_sig", [P, 2, KC])
        cT = sb("cT", [P, KC, 32])
        adaln = sb("adaln", [P, 12, 4, 2])
        mod = sb("mod", [P, 2, KC, 2])
        stat = sb("stat", [P, 3, 32])
        wr = sb("wr", [P, 2, KC, 20])
        br = sb("br", [20, 2])
        head_gain = sb("head_gain", [P, 2])
        qkn_g = sb("qkn_g", [P, 2, DQK])
        lam_in = sb("lam_in", [P, 4, DQK])
        lam = sb("lam", [P, 8])
        ssq = sb("ssq", [P, T * HEADS])
        bank = [ctx.enter_context(nc.psum_tensor(f"bank{b}", [P, 512], F32)) for b in range(8)]

        def const(name):
            return con[:, CONST[name][0]:CONST[name][1]]

        mask_stage = gates[:, :, :].rearrange("p c d -> p (c d)")[:, 0:(2 * LEVELS + 1) * P]
        ident, tri, iota, ones = const("ident"), const("tri"), const("iota"), const("ones")
        selcol = const("selcol")
        rope = const("rope").rearrange("p (t s n) -> p t s n", t=2, s=2)

        def cols(slot):
            return ring[slot][:, :].rearrange("p (k n) -> p k n", k=KC)

        def head_cols(slot):
            return ring[slot][:, :].rearrange("p (k f n) -> p k f n", k=KC, f=4)

        def down_cols(slot):
            return ring[slot][:, :].rearrange("p (k n) -> p k n", k=4)

        full = [[sem(f"full{n}_{s}") for s in range(RING)] for n in range(2)]
        used = [[sem(f"used{n}_{s}") for s in range(RING)] for n in range(2)]
        own_dve = [sem(f"own_dve{n}") for n in range(2)]
        phase = sem("phase")
        x_in, small_in, c_in, late_in = sem("x_in"), sem("small_in"), sem("c_in"), sem("late_in")
        c_ready, c_sigmoid, zeroed = sem("c_ready"), sem("c_sigmoid"), sem("zeroed")
        small_T, masks_ready = sem("small_T"), sem("masks_ready")
        signals = dict(
            squares=("squares", 0, 6), squares2=("squares", 3, 6),
            mean_ready=("mean", 0, 3), o_mean=("mean", 1, 3), mean2=("mean", 2, 3),
            root=("root", 0, 3), o_root=("root", 1, 3), root2=("root", 2, 3),
            xn_ready=("xn_ready", 0, 6), xn2_ready=("xn_ready", 3, 6),
            xT_done=("xT_done", 0, 24), oT_done=("xT_done", 8, 24), xT2_done=("xT_done", 16, 24),
            uT_act=("uT_act", 0, 12), oT_act=("uT_act", 4, 12), uT2_act=("uT_act", 8, 12),
            uT_dve=("uT_dve", 0, 12), oT_dve=("uT_dve", 4, 12), uT2_dve=("uT_dve", 8, 12),
            mod_raw=("mod_raw", 0, 12), mod_T=("mod_T", 0, 12),
            mod_cols=("mod_cols", 0, 12), mod_ready=("mod_ready", 0, 2), diag=("diag", 0, 8),
            gate_mm=("gate_mm", 0, 8), gate_ready=("gate_ready", 0, 8), out_mm=("out_mm", 0, 6),
            x_updated=("x_updated", 0, 12), logit_mm=("logit_mm", 0, 1), logit_biased=("logit_biased", 0, 1),
            logit_T=("logit_T", 0, 1), group_centred=("group_centred", 0, 1), group_exp=("group_exp", 0, 1),
            expert_centred=("expert_centred", 0, 1), expert_exp=("expert_exp", 0, 1), selected=("selected", 0, 1),
            rank_mm=("rank_mm", 0, 1), h_T=("h_T", 0, 6), h_act=("h_act", 0, 3), h_dve=("h_dve", 0, 3))
        shared = {name: sem(name) for name in sorted({v[0] for v in signals.values()})}
        S = [{k: sem(f"{k}{n}") for k in (
            "passes_ready", "onehot", "onehot2", "shifted", "weighted", "gathered", "xe_act", "xe_dve", "silu",
            "h_ready", "wt_done", "wc_act", "wc_dve", "hT_done", "hT_ready", "oe_ready", "y_ready", "acc_done",
        )} for n in range(2)]
        for n in range(2):
            S[n].update({name: shared[v[0]] for name, v in signals.items()})

        def need(eng, n, name, count):
            _, before, each = signals[name]
            eng.wait_ge(S[n][name], count + before + n * each)

        hg = {k: sem(f"hg_{k}") for k in (
            "states_in", "qzz", "q_ready", "zf_ready", "zb_ready", "v_ready",
            "totals", "kd", "qa_f", "qa_b", "lev_f", "lev_b", "free_f", "free_b", "att", "kbT", "kbT_ready", "state_mm",
            "states", "o_done", "o_out", "silu_g", "g_mm", "gated", "state_out")}
        at = {k: sem(f"at_{k}") for k in (
            "cache_in", "proj", "squares", "meansq", "root", "normed", "turned", "qkT", "v_ready", "k_stage",
            "scores", "negmax", "probs", "diff", "aT", "aT_ready", "av", "o_out", "ssq", "lam_sum", "lam_exp", "lam",
            "ckT", "ckT_ready", "o_ready", "out")}
        y_out = sem("y_out")
        LATE = 16 * 13

        uses_before = [[6, 6, 2, 2, 4, 4], [4, 4, 3, 3, 3, 3]]
        full_before = [[96, 96, 32, 32, 256, 256], [64, 64, 48, 48, 48, 48]]

        def hgrn_memory(stack):
            def t(name, shape, dt=F32):
                return sb("hg_" + name, shape, dt, stack)
            return dict(raw=t("raw", [P, 2, 512]), s0=t("s0", [P, 2 * HEADS, P]), sout=t("sout", [P, 2 * HEADS, P]),
                        q=t("q", [P, 2, TOK]), ff=t("ff", [P, 2, TOK]), kf=t("kf", [P, 2, TOK]),
                        fb=t("fb", [P, 2, TOK]), kb=t("kb", [P, 2, TOK]), kd=t("kd", [P, TOK]),
                        qaf=t("qaf", [P, TOK]), qab=t("qab", [P, TOK]), tf=t("tf", [P, TOK]), tb=t("tb", [P, TOK]),
                        att=t("att", [P, TOK]), v=t("v", [P, 2, T, P]), kbT=t("kbT", [P, 4, P]),
                        s1=t("s1", [P, 2, P]), sg=t("sg", [P, 2, 512]))

        def attn_memory(stack):
            def t(name, shape, dt=F32):
                return sb("at_" + name, shape, dt, stack)
            return dict(raw=t("raw", [P, 2, 512]), qT=t("qT", [P, HEADS, T, P]), kT=t("kT", [P, HEADS, 4, P]),
                        v=t("v", [P, T + 1, D]))

        def moe_memory(stack):
            def t(name, shape, dt=F32):
                return sb("moe_" + name, shape, dt, stack)
            return dict(h=t("h", [P, T, D]), acc=t("acc", [P, T, D]), lT=t("lT", [20, TOK]), lg=t("lg", [P, T, 20]),
                        r=t("r", [P, T, EXPERTS + 2]), w=t("w", [P, T, EXPERTS + 2]), sel=t("sel", [P, T, EXPERTS]),
                        t4=t("t4", [P, 12, T, 4]), t16=t("t16", [P, T, 4, 4]), t1=t("t1", [P, 8, T]),
                        npass=t("npass", [P, 1], I32), nf=t("nf", [P, 8]),
                        g=t("g", [P, T, 2, SLOTS]), gw=t("gw", [P, T, 2, P]), xe=t("xe", [P, KC, P]),
                        sg=t("sg", [P, 2, 256]), hh=t("hh", [P, 2, 256]), hT=t("hT", [P, 2, 2, P]),
                        oe=t("oe", [P, 2, 512]), wc=t("wc", [P, 2, TOK]))

        mem = {}
        for key, make in (("hgrn", hgrn_memory), ("attn", attn_memory), ("moe0", moe_memory)):
            with ExitStack() as stack:
                mem[key] = make(stack)
        mem["moe1"] = mem["moe0"]
        HG, AT, MOE = mem["hgrn"], mem["attn"], mem["moe0"]
        AT["sq"] = xn[:, 0, :].rearrange("p (b n) -> p b n", b=2)
        AT["kp"] = xn[:, 1, :].rearrange("p (b n) -> p b n", b=2)
        AT["ck"] = xn[:, 2, :]
        at_tmp = uT[:, :, :].rearrange("p k t -> p (k t)")
        AT["rt"] = AT["raw"][:, 0, :]
        AT["probs"] = at_tmp[:, 0:1536].rearrange("p (b c n) -> p b c n", b=2, c=2)
        AT["a"] = at_tmp[:, 1536:2304].rearrange("p (b n) -> p b n", b=2)
        AT["aT"] = at_tmp[:, 2304:3072].rearrange("p (b n) -> p b n", b=2)

        def meet(eng, n):
            eng.drain().then_inc(phase, 1)
            eng.wait_ge(phase, 4 * (n + 1))

        def passes(eng, n):
            eng.wait_ge(S[n]["passes_ready"], 1)
            return eng.value_load(MOE["npass"][0:1, 0:1], min_val=1, max_val=6)

        def expert_passes(eng, n, before, body, after=None):
            def whole(p, base):
                before(p)
                body(0, base, True, False)
                with eng.Fori(1, PAIRS - 1) as i:
                    body(i, base + i, False, False)
                body(PAIRS - 1, base + (PAIRS - 1), False, True)
                if after is not None:
                    after(base + (PAIRS - 1))

            whole(0, 0)
            count = passes(eng, n)
            with eng.If(count > 1):
                with eng.Fori(1, count) as p:
                    whole(p, p * PAIRS)
            return count

        block = ctx.enter_context(nc.Block())

        @block.sync
        def _(sp):
            def ada(n, slot, blk, turn):
                if not isinstance(turn, int) or turn > 0:
                    sp.wait_ge(used[n][slot], turn)
                src = a["w_ada"][n].rearrange("(p k) (b n) -> p k b n", k=KC, b=12)
                sp.dma_start(cols(slot), src[:, :, blk, :]).then_inc(full[n][slot], 16)

            def block512(n, slot, w, blk, turn):
                sp.wait_ge(used[n][slot], turn)
                src = w.rearrange("(k p) (b n) -> p k b n", p=P, n=512)
                sp.dma_start(cols(slot), src[:, :, blk, :]).then_inc(full[n][slot], 16)

            def head(h, slot, turn):
                if not isinstance(turn, int) or turn > 0:
                    sp.wait_ge(used[0][slot], turn)
                src = a["hgrn_w_in"][0].rearrange("(k p) (f h n) -> p k f h n", p=P, f=5, h=HEADS)
                for f in range(4):
                    sp.dma_start(head_cols(slot)[:, :, f, :], src[:, :, f, h, :]).then_inc(full[0][slot], 16)

            def experts(n):
                def body(i, it, first, last):
                    for slot, (name, e) in enumerate((("moe_w_gate", 0), ("moe_w_up", 0), ("moe_w_gate", 1),
                                                      ("moe_w_up", 1), ("moe_w_down", 0), ("moe_w_down", 1))):
                        sp.wait_ge(used[n][slot], it + uses_before[n][slot])
                        src = a[name][n, 2 * i + e].rearrange("(k p) n -> p k n", p=P)
                        dst = cols(slot) if slot < 4 else down_cols(slot)
                        sp.dma_start(dst, src).then_inc(full[n][slot], 16)
                return expert_passes(sp, n, lambda p: None, body)

            x_rows = x[:, :, :]
            sp.dma_start(x_rows[:, 0, :], a["x_prompt"][0]).then_inc(x_in, 16)
            sp.dma_start(x_rows[:, 1:3, :], a["x_sample"][0].rearrange("(t p) d -> p t d", p=P)).then_inc(x_in, 16)
            for blk in range(4):
                ada(0, blk, blk, 0)
            head(0, 4, 0)
            head(1, 5, 0)
            block512(0, 2, a["hgrn_w_in"][0], 8, 1)
            block512(0, 3, a["hgrn_w_in"][0], 9, 1)
            with sp.Fori(0, 3) as i:
                for b in range(2):
                    ada(0, b, 4 + 2 * i + b, i + 1)
                for b in range(2):
                    head(2 * i + 2 + b, 4 + b, i + 1)
            for b in range(2):
                ada(0, b, 10 + b, 4)
            for b in range(2):
                block512(0, b, a["hgrn_w_out"][0], b, 5)
            count = experts(0)
            for b in range(4):
                sp.wait_ge(used[0][b], count * PAIRS + uses_before[0][b])
                ada(1, b, b, 0)
            for b in range(2):
                sp.wait_ge(used[0][4 + b], count * PAIRS + uses_before[0][4 + b])
                src = a["attn_w_qkv"][0].rearrange("(k p) (b n) -> p k b n", p=P, n=512)
                sp.dma_start(cols(4 + b), src[:, :, b, :]).then_inc(full[1][4 + b], 16)
            for b in range(4):
                block512(1, b, a["attn_w_qkv"][0], 2 + b, 1)
            for b, (slot, turn) in enumerate(((4, 1), (5, 1), (0, 2), (1, 2), (2, 2), (3, 2), (4, 2), (5, 2))):
                ada(1, slot, 4 + b, turn)
            for b in range(2):
                block512(1, b, a["attn_w_out"][0], b, 3)
            experts(1)
            need(sp, 1, "x_updated", 12)
            sp.dma_start(out["y_prompt"][0], x_rows[:, 0, :]).then_inc(y_out, 16)
            sp.dma_start(out["y_sample"][0].rearrange("(t p) d -> p t d", p=P), x_rows[:, 1:3, :]).then_inc(y_out, 16)
            sp.wait_ge(y_out, 32)

        @block.tensor
        def _(pe):
            mm = nc.tensor.matmul

            def ada_block(n, slot, turn, to):
                pe.wait_ge(full[n][slot], 16 * (turn + 1))
                for r in range(2):
                    for g in range(4):
                        last = mm(bank[to][32 * g:32 * g + 32, :], cT[:, 2 * g + r, :], cols(slot)[:, 2 * g + r, :],
                                  start=(r == 0), stop=(r == 1))
                last.then_inc(used[n][slot], 1)

            def turn_mod(n, blk, raw, b, to, count):
                need(pe, n, "mod_raw", count)
                for j in range(4):
                    last = mm(bank[to][:, 2 * j:2 * j + 2], raw[:, b, j * P:(j + 1) * P], selcol, start=True, stop=True)
                last.then_inc(S[n]["mod_T"], 1)

            def modulation(n, raw, blocks, pair=(6, 7)):
                for i, (blk, slot, turn) in enumerate(blocks):
                    if blk >= 4:
                        need(pe, n, "mod_raw", blk - 3)
                    ada_block(n, slot, turn, blk % 4)
                    if i >= 1:
                        last_turn(n, blk - 1, raw, pair)
                last_turn(n, blk, raw, pair)

            def last_turn(n, blk, raw, pair):
                if blk >= 2:
                    need(pe, n, "mod_cols", blk - 1)
                turn_mod(n, blk, raw, blk % 2, pair[blk % 2], blk + 1)

            def gate(n, raw, which):
                for q in range(4):
                    need(pe, n, "diag", 4 * which + q + 1)
                    mm(bank[q][:, :], ones, raw[:, q % 2, :], start=True, stop=True).then_inc(S[n]["gate_mm"], 1)

            def to_features(n, src, ready, count, name, banks=(0, 1, 2, 3)):
                done, act, dve = {"x": ("xT_done", "uT_act", "uT_dve"), "x2": ("xT2_done", "uT2_act", "uT2_dve"),
                                  "o": ("oT_done", "oT_act", "oT_dve")}[name]
                if isinstance(ready, str):
                    need(pe, n, ready, count)
                else:
                    pe.wait_ge(ready, count)
                for k in range(KC):
                    if k >= 4:
                        need(pe, n, act if k % 2 == 0 else dve, (k - 4) // 2 + 1)
                    for t in range(T):
                        last = nc.tensor.transpose(bank[banks[k % 4]][:, t * P:(t + 1) * P],
                                                   src[:, t, k * P:(k + 1) * P], ident)
                    last.then_inc(S[n][done], 1)

            def w_out(n, turn):
                need(pe, n, "oT_act", 4)
                need(pe, n, "oT_dve", 4)
                for half in range(2):
                    pe.wait_ge(full[n][half], 16 * (turn + 1))
                    for t in range(T):
                        m = 3 * half + t
                        if m >= 2:
                            need(pe, n, "x_updated", m - 1)
                        for k in range(KC):
                            last = mm(bank[4 + m % 2][:, :], uT[:, k, t * P:(t + 1) * P], cols(half)[:, k, :],
                                      start=(k == 0), stop=(k == KC - 1))
                        last.then_inc(S[n]["out_mm"], 1)
                    nc.tensor.drain().then_inc(used[n][half], 1)

            def experts(n):
                s = S[n]
                m = MOE
                to_features(n, xn, "xn2_ready", T, "x2")
                need(pe, n, "uT2_act", 4)
                need(pe, n, "uT2_dve", 4)
                for k in range(KC):
                    last = mm(bank[4][0:20, 0:TOK], wr[:, n, k, :], uT[:, k, :], start=(k == 0), stop=(k == KC - 1))
                last.then_inc(s["logit_mm"], 1)
                for t in range(T):
                    for half in range(2):
                        q = 2 * t + half
                        if q >= 4:
                            need(pe, n, "h_act" if q % 2 == 0 else "h_dve", (q - 4) // 2 + 1)
                        for k in range(4):
                            last = nc.tensor.transpose(bank[q % 4][:, k * P:(k + 1) * P],
                                                       uT[:, 4 * half + k, t * P:(t + 1) * P], ident)
                        last.then_inc(s["h_T"], 1)
                need(pe, n, "logit_biased", 1)
                for t in range(T):
                    last = nc.tensor.transpose(bank[5][:, 20 * t:20 * t + 20], m["lT"][:, t * P:(t + 1) * P],
                                               ident[0:20, 0:20])
                last.then_inc(s["logit_T"], 1)
                need(pe, n, "selected", 1)
                for t in range(T + 1):
                    for j in range(min(t + 1, T)):
                        last = mm(bank[6][:, 16 * t:16 * t + 16], tri if j == t else ones, m["sel"][:, j, :],
                                  start=(j == 0), stop=(j == min(t, T - 1)))
                last.then_inc(s["rank_mm"], 1)
                need(pe, n, "h_act", 3)
                need(pe, n, "h_dve", 3)
                pe.wait_ge(s["passes_ready"], 1)

                def full_slot(slot, it):
                    pe.wait_ge(full[n][slot], it * 16 + (full_before[n][slot] + 16))

                def gather(half, it):
                    if half == 0:
                        pe.wait_ge(s["onehot"], it + 1)
                        pe.wait_ge(s["wc_act"], it)
                    else:
                        pe.wait_ge(s["wc_dve"], it)
                    for k in range(4):
                        for t in range(T):
                            last = mm(bank[half][:, k * P:(k + 1) * P],
                                      m["h"][:, t, (4 * half + k) * P:(4 * half + k + 1) * P],
                                      m["g"][:, t, :, :], start=(t == 0), stop=(t == T - 1))
                    last.then_inc(s["gathered"], 1)

                def gate_up(e, part, it):
                    slot = 2 * e + part
                    full_slot(slot, it)
                    for k in range(KC):
                        for g in range(2):
                            last = mm(bank[2 + e][64 * g:64 * g + 64, 256 * part:256 * part + 256],
                                      m["xe"][:, k, 64 * e:64 * e + 64],
                                      cols(slot)[:, k, 256 * g:256 * g + 256],
                                      start=(k == 0), stop=(k == KC - 1))
                    last.then_inc(used[n][slot], 1)

                def combine(t, it):
                    if t == 0:
                        pe.wait_ge(s["wc_act"], it + 1)
                        pe.wait_ge(s["wc_dve"], it + 1)
                        pe.wait_ge(s["oe_ready"], it * 2 + 2)
                    pe.wait_ge(s["acc_done"], it * 6 + 2 * t)
                    for e in range(2):
                        for half in range(2):
                            last = mm(bank[6 + half][:, :], m["wc"][64 * half:64 * half + 64, e, t * P:(t + 1) * P],
                                      m["oe"][64 * half:64 * half + 64, e, :], start=(e == 0), stop=(e == 1))
                    last.then_inc(s["y_ready"], 1)

                def weighted(e):
                    for t in range(T):
                        last = nc.tensor.transpose(bank[e][:, t * P:(t + 1) * P], m["gw"][:, t, e, :], ident)
                    last.then_inc(s["wt_done"], 1)

                def down(e, it):
                    full_slot(4 + e, it)
                    for g in range(2):
                        for j in range(2):
                            for half in range(2):
                                last = mm(bank[5 - e][64 * half:64 * half + 64, :],
                                          m["hT"][:, e, j, 64 * g:64 * g + 64],
                                          down_cols(4 + e)[:, 2 * g + j, 512 * half:512 * half + 512],
                                          start=(g == 0 and j == 0), stop=(g == 1 and j == 1))
                    last.then_inc(used[n][4 + e], 1)

                def body(i, it, first, last):
                    pe.wait_ge(s["xe_act"], it + 1)
                    pe.wait_ge(s["xe_dve"], it + 1)
                    gate_up(0, 0, it)
                    if not first:
                        combine(0, it - 1)
                    gate_up(0, 1, it)
                    if not first:
                        combine(1, it - 1)
                    gate_up(1, 0, it)
                    if not first:
                        combine(2, it - 1)
                    pe.wait_ge(s["weighted"], it + 1)
                    weighted(0)
                    weighted(1)
                    gate_up(1, 1, it)
                    if not last:
                        gather(0, it + 1)
                    pe.wait_ge(s["h_ready"], it * 2 + 2)
                    for e in range(2):
                        for j in range(2):
                            turned = nc.tensor.transpose(bank[4][:, 256 * e + j * P:256 * e + (j + 1) * P],
                                                         m["hh"][:, e, j * P:(j + 1) * P], ident)
                    turned.then_inc(s["hT_done"], 1)
                    if not last:
                        gather(1, it + 1)
                    pe.wait_ge(s["hT_ready"], it + 1)
                    down(0, it)
                    down(1, it)

                def before(p):
                    base = p * PAIRS
                    gather(0, base)
                    gather(1, base)

                def after(it):
                    for t in range(T):
                        combine(t, it)

                expert_passes(pe, n, before, body, after)

            pe.wait_ge(small_in, 64)
            nc.tensor.transpose(bank[4][:, 0:32], small_rows[:, :], ident[0:32, 0:32])
            nc.tensor.transpose(bank[4][:, 32:128], bias_rows[:, :], ident[0:96, 0:96]).then_inc(small_T, 1)
            pe.wait_ge(c_ready, 1)
            raw = HG["raw"]
            modulation(0, raw, [(b, b, 0) for b in range(4)])
            to_features(0, xn, "xn_ready", T, "x")

            def proj(h, b, turn, part):
                w = head_cols(4 + b)
                if part == 0:
                    pe.wait_ge(full[0][4 + b], turn * 64 + 64)
                if part < 6:
                    f = (0, 2, 3)[part // 2]
                    to = bank[part // 2]
                    if part % 2 == 0:
                        pe.wait_ge((hg["q_ready"], hg["zf_ready"], hg["zb_ready"])[part // 2], h)
                    for k in range(4 * (part % 2), 4 * (part % 2) + 4):
                        last = mm(to[:, 0:TOK], w[:, k, f, :], uT[:, k, :], start=(k == 0), stop=(k == KC - 1))
                    if part % 2 == 1:
                        last.then_inc(hg["qzz"], 1)
                else:
                    if part == 6:
                        pe.wait_ge(hg["v_ready"], h)
                    for t in ((0, 1) if part == 6 else (2,)):
                        for k in range(KC):
                            last = mm(bank[3][:, t * P:(t + 1) * P], uT[:, k, t * P:(t + 1) * P], w[:, k, 1, :],
                                      start=(k == 0), stop=(k == KC - 1))
                    if part == 7:
                        last.then_inc(used[0][4 + b], 1)

            def tiles3(to, lhs, rhs):
                for t in range(T):
                    last = mm(to[:, t * P:(t + 1) * P], lhs[:, t * P:(t + 1) * P], rhs[:, t * P:(t + 1) * P],
                              start=True, stop=True)
                return last

            def blocks3(to, lhs, rhs, size):
                for t in range(T):
                    for g in range(P // size):
                        here = slice(t * P + g * size, t * P + (g + 1) * size)
                        last = mm(to[g * size:(g + 1) * size, here], lhs[:, here], rhs[:, here], start=True, stop=True)
                return last

            def level(to, lhs, rhs, n, full):
                size = max(32, 2 << n)
                return tiles3(to, lhs, rhs) if full or size == P else blocks3(to, lhs, rhs, size)

            def scan(h, b, turn, following, before):
                q, kf, kb = HG["q"][:, b, :], HG["kf"][:, b, :], HG["kb"][:, b, :]
                pe.wait_ge(hg["q_ready"], h + 1)
                pe.wait_ge(hg["kd"], h + 1)
                pe.wait_ge(hg["free_f"], h * 8)
                tiles3(bank[4], HG["kd"], q).then_inc(hg["lev_f"], 1)
                if before is not None:
                    turn_mod(0, None, raw, 1 - b, 6, before + 5)
                if following:
                    following(0)
                for n in range(LEVELS):
                    pe.wait_ge(hg["qa_f"], h * 8 + (n + 1))
                    pe.wait_ge(hg["free_f"], h * 8 + (n + 1))
                    level(bank[4], kf, HG["qaf"], n, False).then_inc(hg["lev_f"], 1)
                    pe.wait_ge(hg["qa_b"], h * 8 + (n + 1))
                    if n == 0:
                        pe.wait_ge(hg["att"], h)
                    else:
                        pe.wait_ge(hg["free_b"], h * 6 + n)
                    level(bank[5], kb, HG["qab"], n, n == 0).then_inc(hg["lev_b"], 1)
                    if following:
                        following(n + 1)
                pe.wait_ge(hg["qa_f"], h * 8 + 8)
                pe.wait_ge(hg["qa_b"], h * 8 + 8)
                need(pe, 0, "mod_cols", h + 4)
                for n, (k, t) in enumerate(((kf, 0), (kb, 0), (kf, 1), (kb, 2))):
                    last = nc.tensor.transpose(bank[6][:, n * P:(n + 1) * P], k[:, t * P:(t + 1) * P], ident)
                last.then_inc(hg["kbT"], 1)
                pe.wait_ge(hg["kbT_ready"], h + 1)
                pe.wait_ge(hg["v_ready"], h + 1)
                for n, t in enumerate((0, 0, 1, 2)):
                    last = mm(bank[6][:, n * P:(n + 1) * P], HG["kbT"][:, n, :], HG["v"][:, b, t, :], start=True, stop=True)
                last.then_inc(hg["state_mm"], 1)
                pe.wait_ge(hg["att"], h + 1)
                pe.wait_ge(hg["o_out"], h)
                mm(bank[7][:, 0:P], HG["att"][:, 0:P], HG["v"][:, b, 0, :], start=True, stop=True)
                pe.wait_ge(hg["states"], h + 1)
                for t, (sf, sbk) in ((1, (HG["s0"][:, h, :], HG["s1"][:, 1, :])),
                                     (2, (HG["s1"][:, 0, :], HG["s0"][:, h + HEADS, :]))):
                    to, here = bank[7][:, t * P:(t + 1) * P], slice(t * P, (t + 1) * P)
                    mm(to, HG["att"][:, here], HG["v"][:, b, t, :], start=True, stop=False)
                    mm(to, HG["qaf"][:, here], sf, start=False, stop=False)
                    last = mm(to, HG["qab"][:, here], sbk, start=False, stop=True)
                last.then_inc(hg["o_done"], 1)
                ada_block(0, b, turn + 1, 6)

            need(pe, 0, "uT_act", 4)
            need(pe, 0, "uT_dve", 4)
            need(pe, 0, "mod_ready", 1)
            pe.wait_ge(hg["states_in"], 16)
            for part in range(8):
                proj(0, 0, 0, part)
            scan(0, 0, 0, lambda part: proj(1, 1, 0, part), None)
            scan(1, 1, 0, lambda part: proj(2, 0, 1, part), 0)
            with pe.Fori(1, 3) as i:
                scan(i * 2, 0, i, lambda part: proj(i * 2 + 1, 1, i, part), i * 2 - 1)
                scan(i * 2 + 1, 1, i, lambda part: proj(i * 2 + 2, 0, i + 1, part), i * 2)
            scan(6, 0, 3, lambda part: proj(7, 1, 3, part), 5)
            scan(7, 1, 3, None, 6)
            turn_mod(0, 11, raw, 1, 6, 12)

            for half in range(2):
                pe.wait_ge(full[0][2 + half], 32)
                for t in range(T):
                    m = 3 * half + t
                    if m >= 2:
                        pe.wait_ge(hg["silu_g"], m - 1)
                    for k in range(KC):
                        last = mm(bank[4 + m % 2][:, :], uT[:, k, t * P:(t + 1) * P], cols(2 + half)[:, k, :],
                                  start=(k == 0), stop=(k == KC - 1))
                    last.then_inc(hg["g_mm"], 1)
            nc.tensor.drain().then_inc(used[0][2], 1)
            nc.tensor.drain().then_inc(used[0][3], 1)
            pe.wait_ge(late_in, LATE)
            gate(0, raw, 0)
            need(pe, 0, "gate_ready", 4)
            to_features(0, xn, hg["gated"], 6, "o")
            w_out(0, 5)
            need(pe, 0, "x_updated", 6)
            gate(0, raw, 1)
            need(pe, 0, "gate_ready", 8)
            meet(pe, 0)
            experts(0)
            meet(pe, 1)

            raw = AT["raw"]
            modulation(1, raw, [(b, b, 0) for b in range(4)])
            to_features(1, xn, "xn_ready", T, "x")
            need(pe, 1, "uT_act", 4)
            need(pe, 1, "uT_dve", 4)
            need(pe, 1, "mod_ready", 1)

            def turn_heads(m):
                pe.wait_ge(at["normed"], m + 1)
                if m >= 2:
                    pe.wait_ge(at["qkT"], m - 1)
                src = AT["kp"][:, (m // 3) % 2, :] if m >= 6 and m % 3 == 0 else AT["sq"][:, m % 2, :]
                for j in range(4):
                    last = nc.tensor.transpose(bank[6 + m % 2][:, j * P:(j + 1) * P], src[:, j * P:(j + 1) * P], ident)
                last.then_inc(at["turned"], 1)

            for m, slot in enumerate((4, 5, 0, 1, 2, 3)):
                pe.wait_ge(full[1][slot], 16 if slot >= 4 else 32)
                for t in range(T):
                    b = 3 * m + t
                    if b >= 2:
                        if b - 2 < 12:
                            pe.wait_ge(at["normed"], b - 1)
                        else:
                            pe.wait_ge(at["v_ready"], b - 2 - 12 + 1)
                    for k in range(KC):
                        last = mm(bank[b % 2][:, :], uT[:, k, t * P:(t + 1) * P], cols(slot)[:, k, :],
                                  start=(k == 0), stop=(k == KC - 1))
                    last.then_inc(at["proj"], 1)
                    if 1 <= b <= 12:
                        turn_heads(b - 1)
                nc.tensor.drain().then_inc(used[1][slot], 1)
            pe.wait_ge(at["v_ready"], 6)
            pe.wait_ge(at["qkT"], 12)
            modulation(1, raw, [(4 + b, slot, turn) for b, (slot, turn) in enumerate(
                ((4, 1), (5, 1), (0, 2), (1, 2), (2, 2), (3, 2), (4, 2), (5, 2)))])
            pe.wait_ge(at["cache_in"], 32)
            need(pe, 1, "mod_cols", 12)
            for half in range(2):
                for j in range(4):
                    h = 4 * half + j
                    last = nc.tensor.transpose(bank[6 + half][:, j * P:(j + 1) * P], AT["ck"][:, h * P:(h + 1) * P], ident)
                last.then_inc(at["ckT"], 1)
            gate(1, raw, 0)
            need(pe, 1, "gate_ready", 4)
            need(pe, 1, "mod_ready", 2)
            pe.wait_ge(at["ckT_ready"], 2)

            units = [(h, t) for h in range(HEADS) for t in range(T)]

            def key_tiles(t):
                return (0, 1) if t == 0 else (1, 4)

            def scores(u):
                h, t = units[u]
                lo, hi = key_tiles(t)
                if u >= 2:
                    pe.wait_ge(at["probs"], u - 1)
                for c in range(2):
                    last = mm(bank[2 * (u % 2) + c][:, 0:(hi - lo) * P], AT["qT"][64 * c:64 * c + 64, h, t, :],
                              AT["kT"][64 * c:64 * c + 64, h, lo:hi, :], start=True, stop=True)
                last.then_inc(at["scores"], 1)

            def turn_probs(u):
                h, t = units[u]
                lo, hi = key_tiles(t)
                pe.wait_ge(at["diff"], u + 1)
                for j in range(hi - lo):
                    last = nc.tensor.transpose(bank[4 + u % 2][:, j * P:(j + 1) * P],
                                               AT["a"][:, u % 2, j * P:(j + 1) * P], ident)
                last.then_inc(at["aT"], 1)

            def attend(u):
                h, t = units[u]
                lo, hi = key_tiles(t)
                pe.wait_ge(at["aT_ready"], u + 1)
                if u >= 2:
                    pe.wait_ge(at["o_out"], u - 1)
                for j in range(hi - lo):
                    last = mm(bank[6 + u % 2][:, 0:P], AT["aT"][:, u % 2, j * P:(j + 1) * P],
                              AT["v"][:, lo + j, h * P:(h + 1) * P], start=(j == 0), stop=(j == hi - lo - 1))
                last.then_inc(at["av"], 1)

            scores(0)
            for u in range(len(units)):
                if u + 1 < len(units):
                    scores(u + 1)
                if u >= 1:
                    attend(u - 1)
                turn_probs(u)
            attend(len(units) - 1)
            to_features(1, xn, at["o_ready"], T, "o")
            w_out(1, 3)
            need(pe, 1, "x_updated", 6)
            gate(1, raw, 1)
            need(pe, 1, "gate_ready", 8)
            meet(pe, 2)
            experts(1)

        @block.scalar
        def _(act):
            A = nc.scalar.activation

            def squares(n, name):
                for t in range(T):
                    A(xn[:, t, :], x[:, t, :], ACT.Square, accum_out=stat[:, 0, t:t + 1]).then_inc(S[n][name], 1)

            def root(n, ready, name, count=T, row=1):
                need(act, n, ready, 1)
                A(stat[:, 2, 0:count], stat[:, row, 0:count], ACT.Sqrt).then_inc(S[n][name], 1)

            def modulate(n, done, name, banks=(0, 1, 2, 3)):
                for k in range(0, KC, 2):
                    need(act, n, done, k + 1)
                    for c, lo, hi in COND:
                        last = A(uT[:, k, lo * P:hi * P], bank[banks[k % 4]][:, lo * P:hi * P], ACT.Identity,
                                 bias=mod[:, 0, k, c:c + 1], scale=mod[:, 1, k, c:c + 1])
                    last.then_inc(S[n][name], 1)

            def raw_out(n, raw, b, to, slot, uses, turned):
                act.wait_ge(used[n][slot], uses)
                if turned is not None:
                    need(act, n, "mod_T", turned)
                A(raw[:, b, :], bank[to][:, :], ACT.Copy).then_inc(S[n]["mod_raw"], 1)

            def gate_out(n, base, banks=(0, 1, 2, 3)):
                for c in range(2):
                    for half in range(2):
                        q = 2 * c + half
                        need(act, n, "gate_mm", base + q + 1)
                        A(gates[:, c, 512 * half:512 * half + 512], bank[banks[q]][:, :], ACT.Copy)\
                            .then_inc(S[n]["gate_ready"], 1)

            def turned_out(n):
                for k in range(0, KC, 2):
                    need(act, n, "oT_done", k + 1)
                    A(uT[:, k, :], bank[k % 4][:, 0:TOK], ACT.Identity, scale=head_gain[:, n:n + 1])\
                        .then_inc(S[n]["oT_act"], 1)

            def experts(n):
                s, m = S[n], MOE
                squares(n, "squares2")
                root(n, "mean2", "root2")
                modulate(n, "xT2_done", "uT2_act")
                for q in range(0, 6, 2):
                    need(act, n, "h_T", q + 1)
                    A(m["h"][:, q // 2, 0:512], bank[q % 4][:, :], ACT.Copy).then_inc(s["h_act"], 1)
                need(act, n, "group_centred", 1)
                A(m["t4"][:, 1, :, :], m["t4"][:, 0, :, :], ACT.Exp).then_inc(s["group_exp"], 1)
                need(act, n, "expert_centred", 1)
                A(m["t4"][:, 6, :, :], m["t4"][:, 5, :, :], ACT.Exp).then_inc(s["expert_exp"], 1)

                def rows(it):
                    act.wait_ge(s["gathered"], it * 2 + 1)
                    A(m["xe"][:, 0:4, :], bank[0][:, :], ACT.Copy).then_inc(s["xe_act"], 1)

                def body(i, it, first, last):
                    for e in range(2):
                        if e == 1:
                            act.wait_ge(s["wt_done"], it * 2 + 1)
                            A(m["wc"][:, 0, :], bank[0][:, 0:TOK], ACT.Copy).then_inc(s["wc_act"], 1)
                        act.wait_ge(used[n][2 * e + 1], it + (uses_before[n][2 * e + 1] + 1))
                        A(m["sg"][:, e, :], bank[2 + e][:, 0:256], ACT.Silu).then_inc(s["silu"], 1)
                    if not last:
                        rows(it + 1)
                    act.wait_ge(s["hT_done"], it + 1)
                    A(m["hT"][:, :, :, :].rearrange("p e j n -> p (e j n)"), bank[4][:, :], ACT.Copy)\
                        .then_inc(s["hT_ready"], 1)
                    for e in range(2):
                        act.wait_ge(used[n][4 + e], it + (uses_before[n][4 + e] + 1))
                        A(m["oe"][:, e, :], bank[5 - e][:, :], ACT.Copy).then_inc(s["oe_ready"], 1)

                expert_passes(act, n, lambda p: rows(p * PAIRS), body)

            act.dma_start(c_raw[:, 0, :], a["c_ctx"].rearrange("(p k) -> p k", k=KC)).then_inc(c_in, 16)
            act.dma_start(c_raw[:, 1, :], a["c"][0].rearrange("(p k) -> p k", k=KC)).then_inc(c_in, 16)
            act.dma_start(con[:, :], a["const_f"]).then_inc(small_in, 16)
            act.dma_start(small_rows[0:32, :], a["norm_g"].rearrange("l n (k p) -> (l n k) p", p=P)).then_inc(small_in, 16)
            act.dma_start(bias_rows[:, :], a["b_ada"].rearrange("l (k p) -> (l k) p", p=P)).then_inc(small_in, 16)
            act.dma_start(mask_stage, a["const_mask"]).then_inc(small_in, 16)
            act.dma_start(HG["s0"][:, :, :], a["state_hgrn"][0, 0].rearrange("n h p v -> p (n h) v")).then_inc(hg["states_in"], 16)
            for n in range(2):
                act.dma_start(wr[:, n, :, 0:4], a["moe_w_group"][n].rearrange("(k p) e -> p k e", p=P)).then_inc(late_in, 16)
                act.dma_start(wr[:, n, :, 4:20], a["moe_w_expert"][n].rearrange("(k p) e -> p k e", p=P)).then_inc(late_in, 16)
                act.dma_start(br[0:4, n:n + 1], a["moe_b_group"][n].rearrange("(e o) -> e o", o=1)).then_inc(late_in, 16)
                act.dma_start(br[4:20, n:n + 1], a["moe_b_expert"][n].rearrange("(e o) -> e o", o=1)).then_inc(late_in, 16)
            act.dma_start(head_gain[:, 0:1], a["hgrn_onorm_g"].rearrange("o d -> d o")).then_inc(late_in, 16)
            act.dma_start(head_gain[:, 1:2], a["attn_subln_g"].rearrange("o d -> d o")).then_inc(late_in, 16)
            act.dma_start(qkn_g[:, 0, :], a["attn_qn_g"].partition_broadcast(P)[:, 0, :]).then_inc(late_in, 16)
            act.dma_start(qkn_g[:, 1, :], a["attn_kn_g"].partition_broadcast(P)[:, 0, :]).then_inc(late_in, 16)
            act.dma_start(lam_in[:, :, :], a["attn_lambda"][0].partition_broadcast(P)).then_inc(late_in, 16)

            act.wait_ge(c_in, 32)
            A(c_sig[:, :, :], c_raw[:, :, :], ACT.Sigmoid).then_inc(c_sigmoid, 1)
            act.wait_ge(x_in, 32)
            squares(0, "squares")
            root(0, "mean_ready", "root")
            for blk in range(4):
                raw_out(0, HG["raw"], blk % 2, blk, blk, 1, blk - 1 if blk >= 2 else None)
            need(act, 0, "mod_ready", 1)
            modulate(0, "xT_done", "uT_act")

            def head_out(h, b, heads_done):
                act.wait_ge(hg["qzz"], h * 3 + 1)
                if heads_done is not None:
                    act.wait_ge(hg["o_done"], heads_done)
                A(HG["q"][:, b, :], bank[0][:, 0:TOK], ACT.Copy).then_inc(hg["q_ready"], 1)
                act.wait_ge(hg["qzz"], h * 3 + 2)
                A(HG["ff"][:, b, :], bank[1][:, 0:TOK], ACT.Sigmoid)
                A(HG["kf"][:, b, :], bank[1][:, 0:TOK], ACT.Sigmoid, scale=-1.0).then_inc(hg["zf_ready"], 1)
                act.wait_ge(hg["qzz"], h * 3 + 3)
                A(HG["fb"][:, b, :], bank[2][:, 0:TOK], ACT.Sigmoid)
                A(HG["kb"][:, b, :], bank[2][:, 0:TOK], ACT.Sigmoid, scale=-1.0).then_inc(hg["zb_ready"], 1)

            def rest_out(h, b, turn):
                act.wait_ge(hg["kbT"], h + 1)
                A(HG["kbT"][:, :, :], bank[6][:, :], ACT.Copy).then_inc(hg["kbT_ready"], 1)
                raw_out(0, HG["raw"], b, 6, b, turn + 2, h + 3)

            head_out(0, 0, None)
            with act.Fori(0, 3) as i:
                head_out(i * 2 + 1, 1, i * 2)
                rest_out(i * 2, 0, i)
                head_out(i * 2 + 2, 0, i * 2 + 1)
                rest_out(i * 2 + 1, 1, i)
            head_out(7, 1, 6)
            rest_out(6, 0, 3)
            rest_out(7, 1, 3)
            act.wait_ge(hg["states"], 8)
            act.dma_start(out["new_state"][0, 0].rearrange("n h p v -> p (n h) v"), HG["sout"][:, :, :]).then_inc(hg["state_out"], 16)
            root(0, "o_mean", "o_root", 24)
            for m in range(6):
                act.wait_ge(hg["g_mm"], m + 1)
                if m >= 2:
                    act.wait_ge(hg["gated"], m - 1)
                A(HG["sg"][:, m % 2, :], bank[4 + m % 2][:, :], ACT.Silu).then_inc(hg["silu_g"], 1)
            gate_out(0, 0)
            turned_out(0)
            gate_out(0, 4)
            act.wait_ge(hg["state_out"], 16)
            meet(act, 0)
            experts(0)
            meet(act, 1)

            raw = AT["raw"]
            act.dma_start(AT["v"][:, T, :], a["cache_v"][0, 0].rearrange("p h d -> p (h d)")).then_inc(at["cache_in"], 16)
            squares(1, "squares")
            root(1, "mean_ready", "root")
            for blk in range(4):
                raw_out(1, raw, blk % 2, blk, blk, 1, blk - 1 if blk >= 2 else None)
            need(act, 1, "mod_ready", 1)
            modulate(1, "xT_done", "uT_act")
            need(act, 1, "xT_done", 8)
            act.dma_start(AT["ck"], a["cache_k"][0, 0].rearrange("p h c d -> p (h c d)")).then_inc(at["cache_in"], 16)
            for b in range(18):
                act.wait_ge(at["proj"], b + 1)
                if b < 12:
                    if b >= 2:
                        act.wait_ge(at["turned"], b - 1)
                    A(AT["sq"][:, b % 2, :], bank[b % 2][:, :], ACT.Square).then_inc(at["squares"], 1)
                    act.wait_ge(at["meansq"], b + 1)
                    A(stat[:, 2, 0:8], stat[:, 1, 0:8], ACT.Sqrt).then_inc(at["root"], 1)
                else:
                    half, t = divmod(b - 12, T)
                    A(AT["v"][:, t, 512 * half:512 * half + 512], bank[b % 2][:, :], ACT.Copy).then_inc(at["v_ready"], 1)
                if 1 <= b <= 12:
                    m = b - 1
                    part, rest = divmod(m, 6)
                    half, t = divmod(rest, T)
                    act.wait_ge(at["turned"], m + 1)
                    dst = AT["qT"] if part == 0 else AT["kT"]
                    A(dst[:, 4 * half:4 * half + 4, t, :], bank[6 + m % 2][:, :].rearrange("p (j n) -> p j n", j=4),
                      ACT.Copy).then_inc(at["qkT"], 1)
            act.wait_ge(at["v_ready"], 6)
            act.dma_start(out["new_v"][0, 0].rearrange("p h d -> p (h d)"), AT["v"][:, 0, :]).then_inc(at["out"], 16)
            act.dma_start(out["new_k"][0, 0].rearrange("p h c d -> p (h c d)"),
                          AT["kp"][:, :, :].rearrange("p b n -> p (b n)")).then_inc(at["out"], 16)
            for b, (slot, turn) in enumerate(((4, 1), (5, 1), (0, 2), (1, 2), (2, 2), (3, 2), (4, 2), (5, 2))):
                raw_out(1, raw, b % 2, b % 4, slot, turn + 1, b + 3)
            for half in range(2):
                act.wait_ge(at["ckT"], half + 1)
                A(AT["kT"][:, 4 * half:4 * half + 4, T, :], bank[6 + half][:, :].rearrange("p (j n) -> p j n", j=4),
                  ACT.Copy).then_inc(at["ckT_ready"], 1)
            gate_out(1, 0)
            act.wait_ge(at["lam_sum"], 1)
            A(lam[:, 2:4], lam[:, 0:2], ACT.Exp).then_inc(at["lam_exp"], 1)
            units = [(h, t) for h in range(HEADS) for t in range(T)]

            def turned_probs(u):
                n = P if units[u][1] == 0 else 3 * P
                act.wait_ge(at["aT"], u + 1)
                if u >= 2:
                    act.wait_ge(at["av"], u - 1)
                A(AT["aT"][:, u % 2, 0:n], bank[4 + u % 2][:, 0:n], ACT.Copy).then_inc(at["aT_ready"], 1)

            def head_squares(u):
                h, t = units[u]
                act.wait_ge(at["o_out"], u + 1)
                if u >= 8:
                    act.wait_ge(at["ssq"], u - 7)
                A(AT["raw"][:, u // 4 % 2, P * (u % 4):P * (u % 4 + 1)], xn[:, t, h * P:(h + 1) * P], ACT.Square,
                  accum_out=ssq[:, 8 * t + h:8 * t + h + 1]).then_inc(at["ssq"], 1)

            for u, (h, t) in enumerate(units):
                n = P if t == 0 else 3 * P
                act.wait_ge(at["negmax"], u + 1)
                if u >= 2:
                    act.wait_ge(at["diff"], u - 1)
                for c in range(2):
                    last = A(AT["probs"][:, u % 2, c, 0:n], bank[2 * (u % 2) + c][:, 0:n], ACT.Exp,
                             bias=stat[:, 0, 4 * (u % 2) + c:4 * (u % 2) + c + 1], scale=DQK ** -0.5,
                             accum_out=stat[:, 1, 4 * (u % 2) + c:4 * (u % 2) + c + 1])
                last.then_inc(at["probs"], 1)
                if u >= 1:
                    turned_probs(u - 1)
                if u >= 2:
                    head_squares(u - 2)
            turned_probs(len(units) - 1)
            head_squares(len(units) - 2)
            head_squares(len(units) - 1)
            root(1, "o_mean", "o_root", 24)
            turned_out(1)
            gate_out(1, 4)
            act.wait_ge(at["out"], 32)
            meet(act, 2)
            experts(1)

        @block.vector
        def _(dve):
            v = nc.vector
            own = Chain(dve, own_dve[0])

            def mean(n, ready, name):
                need(dve, n, ready, T)
                v.tensor_scalar(stat[:, 1, 0:T], stat[:, 0, 0:T], 1.0 / D, EPS, ALU.mult, ALU.add)\
                    .then_inc(S[n][name], 1)

            def normalise(n, root, name):
                need(dve, n, root, 1)
                own(v.reciprocal(stat[:, 0, 8:8 + T], stat[:, 2, 0:T]))
                for t in range(T):
                    v.tensor_scalar(xn[:, t, :], x[:, t, :], stat[:, 0, 8 + t:9 + t], None, ALU.mult)\
                        .then_inc(S[n][name], 1)

            def block_columns(n, blk, to, count):
                need(dve, n, "mod_T", count)
                here = (bass.ds(blk, 1) if not isinstance(blk, int) else slice(blk, blk + 1))
                bias = bias_col[:, 48 * n:48 * n + 48].rearrange("p (b j) -> p b j", j=4)[:, here, :]
                v.tensor_tensor(adaln[:, here, :, :], bank[to][:, 0:8].rearrange("p (b j c) -> p b j c", b=1, c=2),
                                bias.unsqueeze(3).broadcast_to([P, 1, 4, 2]), ALU.add).then_inc(S[n]["mod_cols"], 1)

            parts = adaln[:, :, :, :].rearrange("p (a b) j c -> p a (b j) c", b=2)

            def columns(n, norm, first_part, blocks):
                need(dve, n, "mod_cols", blocks)
                g = small[:, 16 * n + 8 * norm:16 * n + 8 * norm + 8].unsqueeze(2).broadcast_to([P, KC, 2])
                v.tensor_copy(mod[:, 0, :, :], parts[:, first_part, :, :])
                v.scalar_tensor_tensor(mod[:, 1, :, :], parts[:, first_part + 1, :, :], 1.0, g, ALU.add, ALU.mult)\
                    .then_inc(S[n]["mod_ready"], 1)

            def gate_diagonals(n, raw, part, which):
                need(dve, n, "mod_cols", 12)
                need(dve, n, "mod_T", 12)
                for q in range(4):
                    c, half = divmod(q, 2)
                    if q >= 2:
                        need(dve, n, "gate_mm", 4 * which + q - 1)
                    v.tensor_tensor(raw[:, q % 2, :].rearrange("p (j m) -> p j m", j=4),
                                    ident.unsqueeze(1).broadcast_to([P, 4, P]),
                                    parts[:, part, 4 * half:4 * half + 4, c].unsqueeze(2).broadcast_to([P, 4, P]),
                                    ALU.mult).then_inc(S[n]["diag"], 1)

            def modulate(n, done, name):
                for k in range(1, KC, 2):
                    need(dve, n, done, k + 1)
                    for c, lo, hi in COND:
                        last = v.tensor_scalar(uT[:, k, lo * P:hi * P], bank[k % 4][:, lo * P:hi * P],
                                               mod[:, 1, k, c:c + 1], mod[:, 0, k, c:c + 1], ALU.mult, ALU.add)
                    last.then_inc(S[n][name], 1)

            def turned_out(n):
                for k in range(1, KC, 2):
                    need(dve, n, "oT_done", k + 1)
                    v.tensor_scalar(uT[:, k, :], bank[k % 4][:, 0:TOK], head_gain[:, n:n + 1], None, ALU.mult)\
                        .then_inc(S[n]["oT_dve"], 1)

            def update_x(n, tmp):
                for m in range(6):
                    half, t = divmod(m, T)
                    c = 0 if t == 0 else 1
                    here = slice(512 * half, 512 * half + 512)
                    need(dve, n, "out_mm", m + 1)
                    if m >= 2:
                        need(dve, n, "x_updated", m - 1)
                    own(v.tensor_tensor(tmp[:, m % 2, :], bank[4 + m % 2][:, :], gates[:, c, here], ALU.mult))
                    v.tensor_tensor(x[:, t, here], x[:, t, here], tmp[:, m % 2, :], ALU.add).then_inc(S[n]["x_updated"], 1)

            def head_mean(n, sums):
                v.tensor_scalar(stat[:, 1, 0:24], sums, 1.0 / P, EPS, ALU.mult, ALU.add).then_inc(S[n]["o_mean"], 1)

            def head_norm(n, tmp):
                for t in range(T):
                    own(v.tensor_tensor(tmp, xn[:, t, :], xn[:, t, :], ALU.mult))
                    own(v.tensor_reduce(stat[:, 0, 8 * t:8 * t + 8], tmp.rearrange("p (h d) -> p h d", h=HEADS), X_AXIS, ALU.add))
                head_mean(n, stat[:, 0, 0:24])

            def head_norm_end(n, done):
                need(dve, n, "o_root", 1)
                own(v.reciprocal(stat[:, 0, 0:24], stat[:, 2, 0:24]))
                for t in range(T):
                    o = xn[:, t, :].rearrange("p (h d) -> p h d", h=HEADS)
                    r = stat[:, 0, 8 * t:8 * t + 8].unsqueeze(2).broadcast_to([P, HEADS, P])
                    ins = v.tensor_tensor(o, o, r, ALU.mult)
                    if done is not None:
                        ins.then_inc(done, 1)
                    else:
                        own(ins)

            def experts(n):
                s, m = S[n], MOE
                mean(n, "squares2", "mean2")
                normalise(n, "root2", "xn2_ready")
                own(v.memset(m["acc"][:, :, :], 0.0))
                own(v.memset(m["r"][:, :, 16:18], NOT_HERE))
                own(v.memset(m["w"][:, :, 16:18], 0.0))
                modulate(n, "xT2_done", "uT2_dve")
                need(dve, n, "logit_mm", 1)
                v.tensor_scalar(m["lT"][:, :], bank[4][0:20, 0:TOK], br[:, n:n + 1], None, ALU.add).then_inc(s["logit_biased"], 1)
                for q in range(1, 6, 2):
                    need(dve, n, "h_T", q + 1)
                    v.tensor_copy(m["h"][:, q // 2, 512:1024], bank[q % 4][:, :]).then_inc(s["h_dve"], 1)
                need(dve, n, "logit_T", 1)
                own(v.tensor_copy(m["lg"][:, :, :], bank[5][:, 0:60].rearrange("p (t e) -> p t e", t=T)))
                t4, t1, t16 = m["t4"], m["t1"], m["t16"]
                first = const("first").unsqueeze(1).broadcast_to([P, T, 4])

                def b4(a1):
                    return a1.unsqueeze(2).broadcast_to([P, T, 4])

                def first_of(values, top, to, tmp, tmp1):
                    own(v.tensor_tensor(t4[:, tmp, :, :], values, b4(top), ALU.is_equal))
                    own(v.tensor_tensor(t4[:, tmp, :, :], t4[:, tmp, :, :], first, ALU.mult))
                    own(v.tensor_reduce(t1[:, tmp1, :], t4[:, tmp, :, :], X_AXIS, ALU.max))
                    own(v.tensor_tensor(t4[:, to, :, :], t4[:, tmp, :, :], b4(t1[:, tmp1, :]), ALU.is_equal))

                gl = m["lg"][:, :, 0:4]
                own(v.tensor_reduce(t1[:, 0, :], gl, X_AXIS, ALU.max))
                v.tensor_tensor(t4[:, 0, :, :], gl, b4(t1[:, 0, :]), ALU.subtract).then_inc(s["group_centred"], 1)
                first_of(gl, t1[:, 0, :], 2, 3, 1)
                el = m["lg"][:, :, 4:20].rearrange("p t (g j) -> p t j g", g=4)
                for t in range(T):
                    own(v.tensor_tensor(t16[:, t, :, :], el[:, t, :, :],
                                        t4[:, 2, t, :].unsqueeze(1).broadcast_to([P, 4, 4]), ALU.mult))
                own(v.tensor_reduce(t4[:, 4, :, :], t16[:, :, :, :], X_AXIS, ALU.add))
                es = t4[:, 4, :, :]
                own(v.tensor_reduce(t1[:, 2, :], es, X_AXIS, ALU.max))
                v.tensor_tensor(t4[:, 5, :, :], es, b4(t1[:, 2, :]), ALU.subtract).then_inc(s["expert_centred"], 1)
                first_of(es, t1[:, 2, :], 7, 3, 1)
                own(v.scalar_tensor_tensor(t4[:, 8, :, :], t4[:, 7, :, :], -1e30, es, ALU.mult, ALU.add))
                own(v.tensor_reduce(t1[:, 3, :], t4[:, 8, :, :], X_AXIS, ALU.max))
                first_of(t4[:, 8, :, :], t1[:, 3, :], 9, 3, 1)
                own(v.tensor_tensor(t4[:, 9, :, :], t4[:, 9, :, :], t4[:, 7, :, :], ALU.add))
                need(dve, n, "group_exp", 1)
                need(dve, n, "expert_exp", 1)
                own(v.tensor_reduce(t1[:, 4, :], t4[:, 1, :, :], X_AXIS, ALU.add))
                own(v.tensor_tensor(t4[:, 10, :, :], t4[:, 6, :, :], t4[:, 9, :, :], ALU.mult))
                own(v.tensor_reduce(t1[:, 5, :], t4[:, 10, :, :], X_AXIS, ALU.add))
                own(v.tensor_tensor(t1[:, 6, :], t1[:, 4, :], t1[:, 5, :], ALU.mult))
                own(v.reciprocal(t1[:, 7, :], t1[:, 6, :]))
                own(v.tensor_tensor(t4[:, 10, :, :], t4[:, 10, :, :], b4(t1[:, 7, :]), ALU.mult))
                for t in range(T):
                    g = t4[:, 2, t, :].unsqueeze(2).broadcast_to([P, 4, 4])
                    for dst, src in ((m["w"], 10), (m["sel"], 9)):
                        last = v.tensor_tensor(dst[:, t, 0:16].rearrange("p (g j) -> p g j", g=4), g,
                                               t4[:, src, t, :].unsqueeze(1).broadcast_to([P, 4, 4]), ALU.mult)
                last.then_inc(s["selected"], 1)
                need(dve, n, "rank_mm", 1)
                rank = bank[6][:, 0:48].rearrange("p (t e) -> p t e", t=T)
                own(v.scalar_tensor_tensor(m["r"][:, :, 0:16], m["sel"][:, :, :], -NOT_HERE, rank, ALU.mult, ALU.add))
                own(v.tensor_scalar(m["r"][:, :, 0:16], m["r"][:, :, 0:16], NOT_HERE, None, ALU.add))
                own(v.tensor_reduce(m["nf"][:, 0:1], bank[6][:, 48:64], X_AXIS, ALU.max))
                own(v.tensor_scalar(m["nf"][:, 1:6], const("over"), m["nf"][:, 0:1], None, ALU.is_lt))
                own(v.tensor_reduce(m["nf"][:, 6:7], m["nf"][:, 1:6], X_AXIS, ALU.add))
                own(v.tensor_scalar(m["nf"][:, 7:8], m["nf"][:, 6:7], 1.0, None, ALU.add))
                v.tensor_copy(m["npass"][:, :], m["nf"][:, 7:8]).then_inc(s["passes_ready"], 1)

                def onehots(pair):
                    for t in range(T):
                        rr = m["r"][:, t, bass.ds(pair * 2, 2)]
                        last = v.tensor_tensor(m["g"][:, t, :, :], iota[:, 0:SLOTS].unsqueeze(1).broadcast_to([P, 2, SLOTS]),
                                               rr.unsqueeze(2).broadcast_to([P, 2, SLOTS]), ALU.is_equal)
                    last.then_inc(s["onehot"], 1)

                def weights(pair, it):
                    for t in range(T):
                        rr = m["r"][:, t, bass.ds(pair * 2, 2)]
                        last = v.tensor_tensor(m["gw"][:, t, :, :], iota.unsqueeze(1).broadcast_to([P, 2, P]),
                                               rr.unsqueeze(2).broadcast_to([P, 2, P]), ALU.is_equal)
                    last.then_inc(s["onehot2"], 1)
                    dve.wait_ge(s["onehot2"], it + 1)
                    for t in range(T):
                        ww = m["w"][:, t, bass.ds(pair * 2, 2)]
                        last = v.tensor_tensor(m["gw"][:, t, :, :], m["gw"][:, t, :, :],
                                               ww.unsqueeze(2).broadcast_to([P, 2, P]), ALU.mult)
                    last.then_inc(s["weighted"], 1)

                def rows(it):
                    dve.wait_ge(s["gathered"], it * 2 + 2)
                    v.tensor_copy(m["xe"][:, 4:8, :], bank[1][:, :].rearrange("p (k n) -> p k n", k=4)).then_inc(s["xe_dve"], 1)

                def before(p):
                    if not isinstance(p, int):
                        v.tensor_scalar(m["r"][:, :, 0:16], m["r"][:, :, 0:16], float(SLOTS), None, ALU.subtract)\
                            .then_inc(s["shifted"], 1)
                        dve.wait_ge(s["shifted"], p)
                    onehots(0)
                    rows(p * PAIRS)

                def accumulate(t, it):
                    dve.wait_ge(s["y_ready"], it * 3 + (t + 1))
                    for half in range(2):
                        here = m["acc"][:, t, 512 * half:512 * half + 512]
                        v.tensor_tensor(here, here, bank[6 + half][:, :], ALU.add).then_inc(s["acc_done"], 1)

                def body(i, it, first, last):
                    if not last:
                        onehots(i + 1)
                    weights(i, it)
                    for e in range(2):
                        if e == 1:
                            if not first:
                                accumulate(2, it - 1)
                            dve.wait_ge(s["wt_done"], it * 2 + 2)
                            v.tensor_copy(m["wc"][:, 1, :], bank[1][:, 0:TOK]).then_inc(s["wc_dve"], 1)
                        elif not first:
                            accumulate(0, it - 1)
                        dve.wait_ge(used[n][2 * e + 1], it + (uses_before[n][2 * e + 1] + 1))
                        dve.wait_ge(s["silu"], it * 2 + (e + 1))
                        v.tensor_tensor(m["hh"][:, e, :], m["sg"][:, e, :], bank[2 + e][:, 256:512], ALU.mult)\
                            .then_inc(s["h_ready"], 1)
                        if e == 0 and not first:
                            accumulate(1, it - 1)
                    if not last:
                        rows(it + 1)

                def after(it):
                    for t in range(T):
                        accumulate(t, it)

                count = expert_passes(dve, n, before, body, after)
                dve.wait_ge(s["acc_done"], count * (6 * PAIRS))
                for t in range(T):
                    c = 0 if t == 0 else 1
                    for half in range(2):
                        here = slice(512 * half, 512 * half + 512)
                        own(v.tensor_tensor(m["acc"][:, t, here], m["acc"][:, t, here], gates[:, c, here], ALU.mult))
                        v.tensor_tensor(x[:, t, here], x[:, t, here], m["acc"][:, t, here], ALU.add)\
                            .then_inc(s["x_updated"], 1)
                need(dve, n, "x_updated", 12)

            own(v.memset(cT[:, :, :], 0.0))
            dve.wait_ge(c_sigmoid, 1)
            v.tensor_tensor(cT[:, :, 0:2].rearrange("p k c -> p c k"), c_raw[:, :, :], c_sig[:, :, :], ALU.mult)\
                .then_inc(c_ready, 1)
            own(v.memset(HG["att"][:, :], 0.0))
            dve.wait_ge(small_T, 1)
            v.tensor_copy(masks[:, :, :].rearrange("p n t -> p (n t)"), mask_stage).then_inc(masks_ready, 1)
            own(v.tensor_copy(small[:, :], bank[4][:, 0:32]))
            own(v.tensor_copy(bias_col[:, :], bank[4][:, 32:128]))
            mean(0, "squares", "mean_ready")
            normalise(0, "root", "xn_ready")
            for blk in range(4):
                block_columns(0, blk, 6 + blk % 2, blk + 1)
            columns(0, 0, 0, 4)
            need(dve, 0, "mod_ready", 1)
            modulate(0, "xT_done", "uT_dve")
            dve.wait_ge(masks_ready, 1)
            def take(src, m):
                mask = masks[:, m, :].unsqueeze(1).broadcast_to([P, T, P])
                return v.copy_predicated(HG["att"][:, :].rearrange("p (t n) -> p t n", t=T), mask,
                                         src[:, 0:TOK].rearrange("p (t n) -> p t n", t=T))

            def scan(h, b, turn, before):
                kf, ff, q = HG["kf"][:, b, :], HG["ff"][:, b, :], HG["q"][:, b, :]
                tf, qaf = HG["tf"], HG["qaf"]
                dve.wait_ge(used[0][4 + b], turn + 1)
                dve.wait_ge(hg["o_done"], h)
                v.tensor_copy(HG["v"][:, b, :, :], bank[3][:, 0:TOK].rearrange("p (t n) -> p t n", t=T)).then_inc(hg["v_ready"], 1)
                dve.wait_ge(hg["zf_ready"], h + 1)
                v.tensor_tensor(qaf[:, :], q, ff, ALU.mult).then_inc(hg["qa_f"], 1)
                sizes = [TOK >> n for n in range(LEVELS + 1)]
                tot = [ff] + [tf[:, sum(sizes[1:n]):sum(sizes[1:n + 1])] for n in range(1, LEVELS + 1)]

                def total(n):
                    pair = tot[n - 1].rearrange("p (b two) -> p b two", two=2)
                    v.tensor_tensor(tot[n], pair[:, :, 0], pair[:, :, 1], ALU.mult).then_inc(hg["totals"], 1)

                dve.wait_ge(hg["lev_f"], h * 8 + 1)
                if before is not None:
                    block_columns(0, before + 4, 6, before + 5)
                take(bank[4], 2 * LEVELS).then_inc(hg["free_f"], 1)
                for n in range(LEVELS):
                    half, blocks = 1 << n, TOK >> (n + 1)
                    if n >= 1:
                        dve.wait_ge(hg["totals"], h * 7 + n)
                        dve.wait_ge(hg["free_b"], h * 6 + n)
                    else:
                        dve.wait_ge(hg["free_f"], h * 8 + 1)
                    dve.wait_ge(hg["lev_f"], h * 8 + (n + 2))
                    pair = tot[n].rearrange("p (b two) -> p b two", two=2)
                    qv = qaf[:, :].rearrange("p (b two l) -> p b two l", two=2, l=half)
                    kv = kf.rearrange("p (b two l) -> p b two l", two=2, l=half)
                    v.tensor_tensor(qv[:, :, 1, :], qv[:, :, 1, :],
                                    pair[:, :, 0].unsqueeze(2).broadcast_to([P, blocks, half]), ALU.mult)
                    v.tensor_tensor(kv[:, :, 0, :], kv[:, :, 0, :],
                                    pair[:, :, 1].unsqueeze(2).broadcast_to([P, blocks, half]), ALU.mult)\
                        .then_inc(hg["qa_f"], 1)
                    take(bank[4], n).then_inc(hg["free_f"], 1)
                    dve.wait_ge(hg["free_f"], h * 8 + (n + 2))
                    dve.wait_ge(hg["lev_b"], h * 7 + (n + 1))
                    total(n + 1)
                    take(bank[5], LEVELS + n)\
                        .then_inc(hg["free_b"] if n < LEVELS - 1 else hg["att"], 1)
                dve.wait_ge(hg["totals"], h * 7 + 7)
                dve.wait_ge(hg["state_mm"], h + 1)
                dve.wait_ge(hg["qa_b"], h * 8 + 8)
                for d in range(2):
                    v.tensor_copy(HG["sout"][:, h + d * HEADS, :], bank[6][:, d * P:(d + 1) * P])
                own_scan = tot[LEVELS][:, 1:2]
                v.scalar_tensor_tensor(HG["s1"][:, 0, :], HG["s0"][:, h, :], own_scan, bank[6][:, 2 * P:3 * P],
                                       ALU.mult, ALU.add)
                v.scalar_tensor_tensor(HG["s1"][:, 1, :], HG["s0"][:, h + HEADS, :], HG["tb"][:, 380:381],
                                       bank[6][:, 3 * P:4 * P], ALU.mult, ALU.add).then_inc(hg["states"], 1)
                dve.wait_ge(hg["o_done"], h + 1)
                v.tensor_copy(xn[:, :, bass.ds(h * P, P)], bank[7][:, 0:TOK].rearrange("p (t n) -> p t n", t=T))\
                    .then_inc(hg["o_out"], 1)

            dve.wait_ge(hg["states_in"], 16)
            scan(0, 0, 0, None)
            scan(1, 1, 0, 0)
            with dve.Fori(1, 3) as i:
                scan(i * 2, 0, i, i * 2 - 1)
                scan(i * 2 + 1, 1, i, i * 2)
            scan(6, 0, 3, 5)
            scan(7, 1, 3, 6)
            block_columns(0, 11, 6, 12)
            dve.wait_ge(hg["o_out"], 8)
            dve.wait_ge(late_in, LATE)
            head_norm(0, HG["s0"][:, 0:8, :].rearrange("p h d -> p (h d)"))
            head_norm_end(0, None)
            for m in range(6):
                half, t = divmod(m, T)
                here = xn[:, t, 512 * half:512 * half + 512]
                dve.wait_ge(hg["silu_g"], m + 1)
                v.tensor_tensor(here, here, HG["sg"][:, m % 2, :], ALU.mult).then_inc(hg["gated"], 1)
            gate_diagonals(0, HG["raw"], 2, 0)
            columns(0, 1, 3, 12)
            turned_out(0)
            need(dve, 0, "gate_ready", 4)
            update_x(0, HG["sg"])
            gate_diagonals(0, HG["raw"], 5, 1)
            meet(dve, 0)
            experts(0)
            meet(dve, 1)
            own = Chain(dve, own_dve[1])

            mean(1, "squares", "mean_ready")
            normalise(1, "root", "xn_ready")
            for blk in range(4):
                block_columns(1, blk, 6 + blk % 2, blk + 1)
            columns(1, 0, 0, 4)
            need(dve, 1, "mod_ready", 1)
            modulate(1, "xT_done", "uT_dve")
            lt = AT["rt"][:, 0:2 * DQK].rearrange("p (n d) -> p n d", n=2)
            l4 = lam_in[:, :, :].rearrange("p (n two) d -> p n two d", two=2)
            own(v.tensor_tensor(lt, l4[:, :, 0, :], l4[:, :, 1, :], ALU.mult))
            v.tensor_reduce(lam[:, 0:2], lt, X_AXIS, ALU.add).then_inc(at["lam_sum"], 1)
            own(v.tensor_scalar(head_gain[:, 1:2], head_gain[:, 1:2], 1.0 - LAM_INIT, None, ALU.mult))
            groups = 512 // DQK

            def by_group(ap):
                return ap.rearrange("p (g d) -> p g d", d=DQK)

            for b in range(12):
                part, rest = divmod(b, 6)
                half, t = divmod(rest, T)
                sq = AT["sq"][:, b % 2, :]
                stage = AT["kp"][:, half, :] if part == 1 and t == 0 else sq
                dve.wait_ge(at["squares"], b + 1)
                own(v.tensor_reduce(stat[:, 0, 0:groups], by_group(sq), X_AXIS, ALU.add))
                v.tensor_scalar(stat[:, 1, 0:groups], stat[:, 0, 0:groups], 1.0 / DQK, EPS, ALU.mult, ALU.add)\
                    .then_inc(at["meansq"], 1)
                dve.wait_ge(at["root"], b + 1)
                own(v.reciprocal(stat[:, 0, 8:8 + groups], stat[:, 2, 0:groups]))
                own(v.tensor_tensor(by_group(stage), by_group(bank[b % 2][:, :]),
                                    stat[:, 0, 8:8 + groups].unsqueeze(2).broadcast_to([P, groups, DQK]), ALU.mult))
                last = v.tensor_tensor(by_group(stage), by_group(stage),
                                       qkn_g[:, part, :].unsqueeze(1).broadcast_to([P, groups, DQK]), ALU.mult)
                if t > 0:
                    own(last)
                    rt = AT["rt"][:, :]
                    sv = stage.rearrange("p (g r h j) -> p g r h j", r=2, h=2, j=16)
                    rv = rt.rearrange("p (g r h j) -> p g r h j", r=2, h=2, j=16)
                    sin = rope[:, t - 1, 1, :].rearrange("p (r h j) -> p r h j", r=2, h=2)
                    for r in range(2):
                        for h in range(2):
                            last = v.tensor_tensor(rv[:, :, r, h, :], sv[:, :, r, 1 - h, :],
                                                   sin[:, r, h, :].unsqueeze(1).broadcast_to([P, groups, 16]), ALU.mult)
                    own(last)
                    own(v.tensor_tensor(by_group(stage), by_group(stage),
                                        rope[:, t - 1, 0, :].unsqueeze(1).broadcast_to([P, groups, DQK]), ALU.mult))
                    last = v.tensor_tensor(stage, stage, rt, ALU.add)
                last.then_inc(at["normed"], 1)
            for blk in range(4, 12):
                block_columns(1, blk, 6 + blk % 2, blk + 1)
            columns(1, 1, 3, 12)
            gate_diagonals(1, AT["raw"], 2, 0)
            dve.wait_ge(at["lam_exp"], 1)
            own(v.tensor_tensor(lam[:, 4:5], lam[:, 2:3], lam[:, 3:4], ALU.subtract))
            own(v.tensor_scalar(lam[:, 5:6], lam[:, 4:5], LAM_INIT, -1.0, ALU.add, ALU.mult))
            units = [(h, t) for h in range(HEADS) for t in range(T)]

            def maxima(u):
                n = P if units[u][1] == 0 else 3 * P
                e = 4 * (u % 2)
                dve.wait_ge(at["scores"], u + 1)
                for c in range(2):
                    last = v.tensor_reduce(stat[:, 2, e + c:e + c + 1], bank[2 * (u % 2) + c][:, 0:n], X_AXIS, ALU.max)
                own(last)
                v.tensor_scalar(stat[:, 0, e:e + 2], stat[:, 2, e:e + 2], -DQK ** -0.5, None, ALU.mult)\
                    .then_inc(at["negmax"], 1)

            def difference(u):
                n = P if units[u][1] == 0 else 3 * P
                e = 4 * (u % 2)
                probs = AT["probs"][:, u % 2, :, 0:n]
                dve.wait_ge(at["probs"], u + 1)
                if u >= 2:
                    dve.wait_ge(at["o_out"], u - 1)
                own(v.reciprocal(stat[:, 2, 16 + e:18 + e], stat[:, 1, e:e + 2]))
                own(v.scalar_tensor_tensor(stat[:, 2, 18 + e:19 + e], stat[:, 1, e:e + 1], stat[:, 2, 17 + e:18 + e],
                                           lam[:, 5:6], ALU.mult, ALU.mult))
                if u >= 2:
                    dve.wait_ge(at["aT"], u - 1)
                v.scalar_tensor_tensor(AT["a"][:, u % 2, 0:n], probs[:, 1, :], stat[:, 2, 18 + e:19 + e], probs[:, 0, :],
                                       ALU.mult, ALU.add).then_inc(at["diff"], 1)

            def attended(u):
                h, t = units[u]
                e = 4 * (u % 2)
                dve.wait_ge(at["av"], u + 1)
                v.tensor_scalar(xn[:, t, h * P:(h + 1) * P], bank[6 + u % 2][:, 0:P], stat[:, 2, 16 + e:17 + e], None,
                                ALU.mult).then_inc(at["o_out"], 1)

            dve.wait_ge(at["out"], 32)
            dve.wait_ge(at["ckT_ready"], 2)
            maxima(0)
            for u in range(len(units)):
                if u + 1 < len(units):
                    maxima(u + 1)
                difference(u)
                if u >= 1:
                    attended(u - 1)
            attended(len(units) - 1)
            dve.wait_ge(at["o_out"], len(units))
            dve.wait_ge(at["ssq"], len(units))
            head_mean(1, ssq[:, :])
            head_norm_end(1, at["o_ready"])
            turned_out(1)
            need(dve, 1, "gate_ready", 4)
            update_x(1, AT["qT"][:, 0:3, :, :].rearrange("p h t n -> p (h t n)")[:, 0:D]
                     .rearrange("p (b n) -> p b n", b=2))
            gate_diagonals(1, AT["raw"], 5, 1)
            meet(dve, 2)
            experts(1)

        @block.gpsimd
        def _(pool):
            g = nc.gpsimd

            def scan(h, b):
                q, fb, kb = HG["q"][:, b, :], HG["fb"][:, b, :], HG["kb"][:, b, :]
                pool.wait_ge(hg["o_done"], h)
                pool.wait_ge(hg["zb_ready"], h + 1)
                g.tensor_tensor(HG["kd"][:, :], HG["kf"][:, b, :], kb, ALU.add).then_inc(hg["kd"], 1)
                g.tensor_tensor(HG["qab"][:, :], q, fb, ALU.mult).then_inc(hg["qa_b"], 1)
                tot, lo = fb, 0
                for n in range(LEVELS):
                    half, blocks = 1 << n, TOK >> (n + 1)
                    pool.wait_ge(hg["lev_b"], h * 7 + (n + 1))
                    pair = tot.rearrange("p (b two) -> p b two", two=2)
                    new = HG["tb"][:, lo:lo + blocks]
                    g.tensor_tensor(new, pair[:, :, 0], pair[:, :, 1], ALU.mult)
                    qv = HG["qab"][:, :].rearrange("p (b two l) -> p b two l", two=2, l=half)
                    kv = kb.rearrange("p (b two l) -> p b two l", two=2, l=half)
                    g.tensor_tensor(qv[:, :, 0, :], qv[:, :, 0, :],
                                    pair[:, :, 1].unsqueeze(2).broadcast_to([P, blocks, half]), ALU.mult)
                    g.tensor_tensor(kv[:, :, 1, :], kv[:, :, 1, :],
                                    pair[:, :, 0].unsqueeze(2).broadcast_to([P, blocks, half]), ALU.mult)\
                        .then_inc(hg["qa_b"], 1)
                    tot, lo = new, lo + blocks

            with pool.Fori(0, 4) as i:
                scan(i * 2, 0)
                scan(i * 2 + 1, 1)
            meet(pool, 0)
            meet(pool, 1)
            meet(pool, 2)


_INS = ["x_prompt", "x_sample", "c", "cache_k", "cache_v", "state_hgrn", "c_ctx", "norm_g", "w_ada", "b_ada",
        "hgrn_w_in", "hgrn_onorm_g", "hgrn_w_out", "attn_w_qkv", "attn_qn_g", "attn_kn_g",
        "attn_lambda", "attn_subln_g", "attn_w_out", "moe_w_group", "moe_b_group", "moe_w_expert", "moe_b_expert",
        "moe_w_gate", "moe_w_up", "moe_w_down"]
_OUTS = [("y_prompt", (1, P, D)), ("y_sample", (1, 2 * P, D)), ("new_k", (1, 1, P, HEADS, 2, DQK)),
         ("new_v", (1, 1, P, HEADS, P)), ("new_state", (1, 1, 2, HEADS, P, P))]


def kernel(**inputs):
    import numpy as _np
    import concourse.bacc as _bacc
    from concourse import mybir as _mybir
    from concourse.bass_utils import run_bass_kernel_spmd as _run

    nc = _bacc.Bacc("TRN2", target_bir_lowering=False, num_devices=1)
    const_f, const_mask = shape_constants()
    data = {name: inputs[name] for name in _INS}
    data.update(const_f=const_f, const_mask=const_mask)
    arrays, aps, outs = {}, {}, {}
    for name, value in data.items():
        v = _np.ascontiguousarray(value)
        arrays[f"in_{name}"] = v
        aps[name] = nc.dram_tensor(f"in_{name}", v.shape, _mybir.dt.from_np(v.dtype), kind="ExternalInput").ap()
    for name, shape in _OUTS:
        outs[name] = nc.dram_tensor(f"out_{name}", shape, _mybir.dt.float32, kind="ExternalOutput").ap()
    trunk(nc, aps, outs)
    r = _run(nc, [arrays], core_ids=[0])
    return tuple(r.results[0][f"out_{name}"] for name, _ in _OUTS)
```
